# Optimizing a Trainium2 kernel written in Bass

```python
import math
import jax
import jax.numpy as jnp
from jax import lax
import numpy as np

D_MODEL = 1024
BATCH = 1
SEQ = 128
DEPTH = 2
DEC_BATCH = 1
DEC_SEQ = 128
PAST_LEN = 128

F32 = jnp.float32
GRID_W = 64
HEAD_DIM = 64
HEADS_PER_GROUP = D_MODEL // (4 * HEAD_DIM)
MIX_WIDTH = 4 * HEADS_PER_GROUP * HEAD_DIM
WIN_HEADS = HEADS_PER_GROUP
WIN_KV_HEADS = WIN_HEADS // 2
WINDOW = 128
BLOCK = 128
DIFF_HEADS = HEADS_PER_GROUP
DIFF_HALF = HEAD_DIM // 2
MLA_HEADS = HEADS_PER_GROUP
MLA_Q_RANK = 3 * D_MODEL // 16
MLA_KV_RANK = D_MODEL // 8
MLA_NOPE = HEAD_DIM
MLA_ROPE = HEAD_DIM // 2
MLA_VDIM = HEAD_DIM
NA_HEADS = HEADS_PER_GROUP
NA_ROWS = 8
NA_COLS = 16
D_FF = ((8 * D_MODEL // 3 + 127) // 128) * 128
N_EXPERTS = 8
TOP_K = 2
D_FF_EXPERT = 7 * D_MODEL // 2
ROPE_THETA = 10000.0
EPS = 1e-6
NEG_INF = -1e30
DENSE_KEY_LIMIT = 2048
Q_BLOCK = 128
IN_SIZES = (WIN_HEADS * HEAD_DIM, WIN_KV_HEADS * HEAD_DIM, WIN_KV_HEADS * HEAD_DIM,
            DIFF_HEADS * HEAD_DIM, DIFF_HEADS * HEAD_DIM, DIFF_HEADS * HEAD_DIM,
            MLA_Q_RANK, MLA_KV_RANK, MLA_ROPE,
            NA_HEADS * HEAD_DIM, NA_HEADS * HEAD_DIM, NA_HEADS * HEAD_DIM)
IN_WIDTH = sum(IN_SIZES)

kernel_name = 'hybrid_diffusion_parallel_heads_step'

def _rmsnorm(x, g):
    x32 = x.astype(F32)
    y = x32 * lax.rsqrt(jnp.mean(x32 * x32, axis=-1, keepdims=True) + EPS)
    return (y * g.astype(F32)).astype(x.dtype)

def _heads(t, n):
    b, l, _ = t.shape
    return t.reshape(b, l, n, -1).transpose(0, 2, 1, 3)

def _merge(o):
    b, h, l, d = o.shape
    return o.transpose(0, 2, 1, 3).reshape(b, l, h * d)

def _project(h, w_in_l):
    pts = []
    acc = 0
    for s in IN_SIZES[:-1]:
        acc += s
        pts.append(acc)
    return jnp.split(h @ w_in_l, pts, axis=-1)

def _rope1d(x, pos):
    d = x.shape[-1]
    inv = ROPE_THETA ** (-jnp.arange(0, d, 2, dtype=F32) / d)
    ang = pos.astype(F32)[:, None] * inv[None, :]
    cos = jnp.concatenate([jnp.cos(ang), jnp.cos(ang)], axis=-1)
    sin = jnp.concatenate([jnp.sin(ang), jnp.sin(ang)], axis=-1)
    rot = jnp.concatenate([-x[..., d // 2:], x[..., :d // 2]], axis=-1)
    return (x.astype(F32) * cos + rot.astype(F32) * sin).astype(x.dtype)

def _rope2d(x, pos_r, pos_c):
    h = x.shape[-1] // 2
    return jnp.concatenate([_rope1d(x[..., :h], pos_r), _rope1d(x[..., h:], pos_c)], axis=-1)

def _sdpa(q, k, v, sink=None):
    scale = q.shape[-1] ** -0.5

    def attend(qb):
        s = jnp.einsum('bhqd,bhkd->bhqk', qb, k).astype(F32) * scale
        if sink is not None:
            sk = jnp.broadcast_to(sink.astype(F32)[None, :, None, None], s.shape[:-1] + (1,))
            s = jnp.concatenate([s, sk], axis=-1)
        p = jax.nn.softmax(s, axis=-1)
        if sink is not None:
            p = p[..., :-1]
        return jnp.einsum('bhqk,bhkd->bhqd', p.astype(v.dtype), v)

    b, h, lq, _ = q.shape
    if k.shape[2] >= DENSE_KEY_LIMIT and lq > Q_BLOCK and lq % Q_BLOCK == 0:
        nb = lq // Q_BLOCK
        qb = q.reshape(b, h, nb, Q_BLOCK, -1).transpose(2, 0, 1, 3, 4)
        o = lax.map(attend, qb)
        return o.transpose(1, 2, 0, 3, 4).reshape(b, h, lq, -1)
    return attend(q)

def _window_attn(q, k, v, kc, vc, sink):
    b, h, n, d = q.shape
    g = k.shape[1]
    r = h // g
    nb = n // BLOCK
    scale = d ** -0.5
    qb = q.reshape(b, g, r, nb, BLOCK, d)
    pad = ((0, 0), (0, 0), (BLOCK, BLOCK), (0, 0))
    kp = jnp.pad(k, pad).reshape(b, g, nb + 2, BLOCK, d)
    vp = jnp.pad(v, pad).reshape(b, g, nb + 2, BLOCK, d)
    kw = jnp.concatenate([kp[:, :, :-2], kp[:, :, 1:-1], kp[:, :, 2:]], axis=3)
    vw = jnp.concatenate([vp[:, :, :-2], vp[:, :, 1:-1], vp[:, :, 2:]], axis=3)
    qi = jnp.arange(BLOCK)[:, None]
    kj = jnp.arange(3 * BLOCK)[None, :]
    kpos = jnp.arange(nb)[:, None, None] * BLOCK - BLOCK + kj[None]
    valid = (jnp.abs(kj - BLOCK - qi) <= WINDOW)[None] & (kpos >= 0) & (kpos < n)
    s_loc = jnp.einsum('bgrnqd,bgnkd->bgrnqk', qb, kw).astype(F32) * scale
    s_loc = jnp.where(valid, s_loc, NEG_INF)
    s_ctx = jnp.einsum('bgrnqd,bgkd->bgrnqk', qb, kc).astype(F32) * scale
    s_sink = jnp.broadcast_to(sink.astype(F32).reshape(g, r)[None, :, :, None, None, None],
                              s_loc.shape[:-1] + (1,))
    p = jax.nn.softmax(jnp.concatenate([s_loc, s_ctx, s_sink], axis=-1), axis=-1)
    w_loc = p[..., :3 * BLOCK].astype(v.dtype)
    w_ctx = p[..., 3 * BLOCK:3 * BLOCK + kc.shape[2]].astype(v.dtype)
    o = (jnp.einsum('bgrnqk,bgnkd->bgrnqd', w_loc, vw)
         + jnp.einsum('bgrnqk,bgkd->bgrnqd', w_ctx, vc))
    return o.reshape(b, h, n, d)

def _neighborhood_attn(q, k, v, kc, vc, rpb):
    b, h, n, d = q.shape
    rows = n // GRID_W
    kh = min(NA_ROWS, rows)
    scale = d ** -0.5
    r = jnp.arange(rows)
    rs = jnp.clip(r - kh // 2, 0, rows - kh)
    row_idx = rs[:, None] + jnp.arange(kh)[None, :]
    col = jnp.arange(GRID_W)
    cs = jnp.clip(col - NA_COLS // 2, 0, GRID_W - NA_COLS)
    col_valid = (col[None, :] >= cs[:, None]) & (col[None, :] < cs[:, None] + NA_COLS)
    rel_r = row_idx - r[:, None] + (NA_ROWS - 1)
    rel_c = jnp.clip(col[None, :] - col[:, None], -(NA_COLS - 1), NA_COLS - 1) + (NA_COLS - 1)
    bias = rpb[:, rel_r[:, None, :, None], rel_c[None, :, None, :]].astype(F32)
    qg = q.reshape(b, h, rows, GRID_W, d)
    k_rows = k.reshape(b, h, rows, GRID_W, d)[:, :, row_idx]
    v_rows = v.reshape(b, h, rows, GRID_W, d)[:, :, row_idx]
    s_loc = jnp.einsum('bhrqd,bhrikd->bhrqik', qg, k_rows).astype(F32) * scale + bias[None]
    s_loc = jnp.where(col_valid[:, None, :], s_loc, NEG_INF).reshape(b, h, rows, GRID_W, kh * GRID_W)
    s_ctx = jnp.einsum('bhrqd,bhkd->bhrqk', qg, kc).astype(F32) * scale
    p = jax.nn.softmax(jnp.concatenate([s_loc, s_ctx], axis=-1), axis=-1)
    w_loc = p[..., :kh * GRID_W].reshape(b, h, rows, GRID_W, kh, GRID_W).astype(v.dtype)
    w_ctx = p[..., kh * GRID_W:].astype(v.dtype)
    o = (jnp.einsum('bhrqik,bhrikd->bhrqd', w_loc, v_rows)
         + jnp.einsum('bhrqk,bhkd->bhrqd', w_ctx, vc))
    return o.reshape(b, h, n, d)

def _diff_out(o1, o2, lam_l, lam_init, subln_l):
    lq1, lk1, lq2, lk2 = lam_l
    lam = (jnp.exp(jnp.sum(lq1.astype(F32) * lk1.astype(F32)))
           - jnp.exp(jnp.sum(lq2.astype(F32) * lk2.astype(F32))) + lam_init)
    o = o1 - lam.astype(o1.dtype) * o2
    return _rmsnorm(o, subln_l) * (1.0 - lam_init)

def _mla_up(ckv_n, wukv_l):
    kv = _heads(ckv_n @ wukv_l, MLA_HEADS)
    return kv[..., :MLA_NOPE], kv[..., MLA_NOPE:]

def _mla_key(k_nope, kpe):
    return jnp.concatenate([k_nope, jnp.broadcast_to(kpe[:, None], k_nope.shape[:3] + (MLA_ROPE,))], axis=-1)

def _mixer_context(h, w_in_l, w_o_l, sink_l, lam_l, lam_init, subln_l, qn_l, kvn_l, wuq_l, wukv_l):
    qa, ka, va, qb, kb, vb, cq, ckv, kpe, qd, kd, vd = _project(h, w_in_l)
    rep = WIN_HEADS // WIN_KV_HEADS
    ka_h, va_h = _heads(ka, WIN_KV_HEADS), _heads(va, WIN_KV_HEADS)
    oa = _sdpa(_heads(qa, WIN_HEADS), jnp.repeat(ka_h, rep, axis=1), jnp.repeat(va_h, rep, axis=1), sink_l)
    qb_h, kb_h, vb_h = _heads(qb, DIFF_HEADS), _heads(kb, DIFF_HEADS), _heads(vb, DIFF_HEADS)
    ob = _diff_out(_sdpa(qb_h[..., :DIFF_HALF], kb_h[..., :DIFF_HALF], vb_h),
                   _sdpa(qb_h[..., DIFF_HALF:], kb_h[..., DIFF_HALF:], vb_h),
                   lam_l, lam_init, subln_l)
    q_c = _heads(_rmsnorm(cq, qn_l) @ wuq_l, MLA_HEADS)
    ckv_n = _rmsnorm(ckv, kvn_l)
    k_nope, v_c = _mla_up(ckv_n, wukv_l)
    oc = _sdpa(q_c, _mla_key(k_nope, kpe), v_c)
    kd_h, vd_h = _heads(kd, NA_HEADS), _heads(vd, NA_HEADS)
    od = _sdpa(_heads(qd, NA_HEADS), kd_h, vd_h)
    out = _merge(jnp.concatenate([oa, ob, oc, od], axis=1)) @ w_o_l
    return out, (ka_h, va_h, kb_h, vb_h, ckv_n, kpe, kd_h, vd_h)

def _mixer_latent(h, cached, w_in_l, w_o_l, sink_l, lam_l, lam_init, subln_l, qn_l, kvn_l, wuq_l, wukv_l, rpb_l):
    ka_c, va_c, kb_c, vb_c, ckv_c, kpe_c, kd_c, vd_c = cached
    n = h.shape[1]
    pos = jnp.arange(n)
    pr, pc = pos // GRID_W, pos % GRID_W
    qa, ka, va, qb, kb, vb, cq, ckv, kpe, qd, kd, vd = _project(h, w_in_l)
    oa = _window_attn(_rope2d(_heads(qa, WIN_HEADS), pr, pc), _rope2d(_heads(ka, WIN_KV_HEADS), pr, pc),
                      _heads(va, WIN_KV_HEADS), ka_c, va_c, sink_l)
    qb_h, kb_h, vb_h = _heads(qb, DIFF_HEADS), _heads(kb, DIFF_HEADS), _heads(vb, DIFF_HEADS)
    q1 = _rope2d(qb_h[..., :DIFF_HALF], pr, pc)
    q2 = _rope2d(qb_h[..., DIFF_HALF:], pr, pc)
    k1 = jnp.concatenate([_rope2d(kb_h[..., :DIFF_HALF], pr, pc), kb_c[..., :DIFF_HALF]], axis=2)
    k2 = jnp.concatenate([_rope2d(kb_h[..., DIFF_HALF:], pr, pc), kb_c[..., DIFF_HALF:]], axis=2)
    v_all = jnp.concatenate([vb_h, vb_c], axis=2)
    ob = _diff_out(_sdpa(q1, k1, v_all), _sdpa(q2, k2, v_all), lam_l, lam_init, subln_l)
    q_c = _heads(_rmsnorm(cq, qn_l) @ wuq_l, MLA_HEADS)
    q_c = jnp.concatenate([q_c[..., :MLA_NOPE], _rope2d(q_c[..., MLA_NOPE:], pr, pc)], axis=-1)
    k_nope, v_lat = _mla_up(_rmsnorm(ckv, kvn_l), wukv_l)
    k_nope_c, v_ctx = _mla_up(ckv_c, wukv_l)
    k_all = jnp.concatenate([_mla_key(k_nope, _rope2d(kpe, pr, pc)), _mla_key(k_nope_c, kpe_c)], axis=2)
    oc = _sdpa(q_c, k_all, jnp.concatenate([v_lat, v_ctx], axis=2))
    od = _neighborhood_attn(_heads(qd, NA_HEADS), _heads(kd, NA_HEADS), _heads(vd, NA_HEADS), kd_c, vd_c, rpb_l)
    return _merge(jnp.concatenate([oa, ob, oc, od], axis=1)) @ w_o_l

def _swiglu(t, wg, wu, wd):
    return (jax.nn.silu(t @ wg) * (t @ wu)) @ wd

def _moe(t, router, wg, wu, wd):
    logits = (t @ router).astype(F32)
    top_v, top_i = lax.top_k(logits, TOP_K)
    gates = jax.nn.softmax(top_v, axis=-1)
    combine = jnp.sum(jax.nn.one_hot(top_i, N_EXPERTS, dtype=F32) * gates[..., None], axis=1)
    out = jnp.zeros_like(t)
    for e in range(N_EXPERTS):
        out = out + combine[:, e:e + 1].astype(t.dtype) * _swiglu(t, wg[e], wu[e], wd[e])
    return out

def _channel_mixer(h, l, ffn_w_gate, ffn_w_up, ffn_w_down, moe_router, moe_w_gate, moe_w_up, moe_w_down):
    i = l // 2
    if l % 2 == 0:
        return _swiglu(h, ffn_w_gate[i], ffn_w_up[i], ffn_w_down[i])
    b, n, d = h.shape
    return _moe(h.reshape(b * n, d), moe_router[i], moe_w_gate[i], moe_w_up[i], moe_w_down[i]).reshape(b, n, d)

def _modulation(silu_cond, w_ada_l, b_ada_l):
    m = (silu_cond @ w_ada_l + b_ada_l)[:, None, :]
    return jnp.split(m, 6, axis=-1)

def setup_inputs(seed: int = 0) -> dict:
    key = jax.random.key(seed)
    ks = iter(jax.random.split(key, 48))
    n_dense = (DEPTH + 1) // 2
    n_moe = DEPTH // 2

    def nrm(shape, scale):
        return jax.random.normal(next(ks), shape, F32) * scale

    def gain(shape):
        return 1.0 + nrm(shape, 0.1)

    return {
        'x_prompt': nrm((BATCH, SEQ, D_MODEL), 1.0),
        'x_sample': nrm((DEC_BATCH, DEC_SEQ, D_MODEL), 1.0),
        'cache_win_k': nrm((DEC_BATCH, DEPTH, WIN_KV_HEADS, PAST_LEN, HEAD_DIM), 1.0),
        'cache_win_v': nrm((DEC_BATCH, DEPTH, WIN_KV_HEADS, PAST_LEN, HEAD_DIM), 1.0),
        'cache_diff_k': nrm((DEC_BATCH, DEPTH, DIFF_HEADS, PAST_LEN, HEAD_DIM), 1.0),
        'cache_diff_v': nrm((DEC_BATCH, DEPTH, DIFF_HEADS, PAST_LEN, HEAD_DIM), 1.0),
        'cache_mla_ckv': nrm((DEC_BATCH, DEPTH, PAST_LEN, MLA_KV_RANK), 1.0),
        'cache_mla_kpe': nrm((DEC_BATCH, DEPTH, PAST_LEN, MLA_ROPE), 1.0),
        'cache_na_k': nrm((DEC_BATCH, DEPTH, NA_HEADS, PAST_LEN, HEAD_DIM), 1.0),
        'cache_na_v': nrm((DEC_BATCH, DEPTH, NA_HEADS, PAST_LEN, HEAD_DIM), 1.0),
        'c': nrm((DEC_BATCH, D_MODEL), 1.0),
        'c_ctx': nrm((D_MODEL,), 1.0),
        'w_ada': nrm((DEPTH, D_MODEL, 6 * D_MODEL), D_MODEL ** -0.5),
        'b_ada': nrm((DEPTH, 6 * D_MODEL), 0.02),
        'norm_mix_pre': gain((DEPTH, D_MODEL)),
        'norm_mix_post': gain((DEPTH, D_MODEL)),
        'norm_ffn_pre': gain((DEPTH, D_MODEL)),
        'norm_ffn_post': gain((DEPTH, D_MODEL)),
        'w_in': nrm((DEPTH, D_MODEL, IN_WIDTH), D_MODEL ** -0.5),
        'w_o': nrm((DEPTH, MIX_WIDTH, D_MODEL), MIX_WIDTH ** -0.5),
        'win_sink': nrm((DEPTH, WIN_HEADS), 1.0),
        'diff_lq1': nrm((DEPTH, DIFF_HALF), 0.1),
        'diff_lk1': nrm((DEPTH, DIFF_HALF), 0.1),
        'diff_lq2': nrm((DEPTH, DIFF_HALF), 0.1),
        'diff_lk2': nrm((DEPTH, DIFF_HALF), 0.1),
        'diff_subln': gain((DEPTH, HEAD_DIM)),
        'mla_q_norm': gain((DEPTH, MLA_Q_RANK)),
        'mla_kv_norm': gain((DEPTH, MLA_KV_RANK)),
        'mla_wuq': nrm((DEPTH, MLA_Q_RANK, MLA_HEADS * (MLA_NOPE + MLA_ROPE)), MLA_Q_RANK ** -0.5),
        'mla_wukv': nrm((DEPTH, MLA_KV_RANK, MLA_HEADS * (MLA_NOPE + MLA_VDIM)), MLA_KV_RANK ** -0.5),
        'na_rpb': nrm((DEPTH, NA_HEADS, 2 * NA_ROWS - 1, 2 * NA_COLS - 1), 0.1),
        'ffn_w_gate': nrm((n_dense, D_MODEL, D_FF), D_MODEL ** -0.5),
        'ffn_w_up': nrm((n_dense, D_MODEL, D_FF), D_MODEL ** -0.5),
        'ffn_w_down': nrm((n_dense, D_FF, D_MODEL), D_FF ** -0.5),
        'moe_router': nrm((n_moe, D_MODEL, N_EXPERTS), D_MODEL ** -0.5),
        'moe_w_gate': nrm((n_moe, N_EXPERTS, D_MODEL, D_FF_EXPERT), D_MODEL ** -0.5),
        'moe_w_up': nrm((n_moe, N_EXPERTS, D_MODEL, D_FF_EXPERT), D_MODEL ** -0.5),
        'moe_w_down': nrm((n_moe, N_EXPERTS, D_FF_EXPERT, D_MODEL), D_FF_EXPERT ** -0.5),
    }

def reference(x_prompt, x_sample, cache_win_k, cache_win_v, cache_diff_k, cache_diff_v,
              cache_mla_ckv, cache_mla_kpe, cache_na_k, cache_na_v, c, c_ctx,
              w_ada, b_ada, norm_mix_pre, norm_mix_post, norm_ffn_pre, norm_ffn_post,
              w_in, w_o, win_sink, diff_lq1, diff_lk1, diff_lq2, diff_lk2, diff_subln,
              mla_q_norm, mla_kv_norm, mla_wuq, mla_wukv, na_rpb,
              ffn_w_gate, ffn_w_up, ffn_w_down, moe_router, moe_w_gate, moe_w_up, moe_w_down):
    silu_ctx = jax.nn.silu(c_ctx)[None]
    silu_lat = jax.nn.silu(c)
    xp, xs = x_prompt, x_sample
    ctx_new = [[] for _ in range(8)]
    for l in range(DEPTH):
        lam_init = 0.8 - 0.6 * math.exp(-0.3 * l)
        lam_l = (diff_lq1[l], diff_lk1[l], diff_lq2[l], diff_lk2[l])
        mix_w = (w_in[l], w_o[l], win_sink[l], lam_l, lam_init, diff_subln[l],
                 mla_q_norm[l], mla_kv_norm[l], mla_wuq[l], mla_wukv[l])
        ffn_w = (ffn_w_gate, ffn_w_up, ffn_w_down, moe_router, moe_w_gate, moe_w_up, moe_w_down)

        sh1, sc1, gt1, sh2, sc2, gt2 = _modulation(silu_ctx, w_ada[l], b_ada[l])
        h = _rmsnorm(xp, norm_mix_pre[l]) * (1.0 + sc1) + sh1
        y, ctx_l = _mixer_context(h, *mix_w)
        xp = xp + gt1 * _rmsnorm(y, norm_mix_post[l])
        h = _rmsnorm(xp, norm_ffn_pre[l]) * (1.0 + sc2) + sh2
        xp = xp + gt2 * _rmsnorm(_channel_mixer(h, l, *ffn_w), norm_ffn_post[l])
        for i, t in enumerate(ctx_l):
            ctx_new[i].append(t)

        cached = (cache_win_k[:, l], cache_win_v[:, l], cache_diff_k[:, l], cache_diff_v[:, l],
                  cache_mla_ckv[:, l], cache_mla_kpe[:, l], cache_na_k[:, l], cache_na_v[:, l])
        sh1, sc1, gt1, sh2, sc2, gt2 = _modulation(silu_lat, w_ada[l], b_ada[l])
        h = _rmsnorm(xs, norm_mix_pre[l]) * (1.0 + sc1) + sh1
        y = _mixer_latent(h, cached, *mix_w, na_rpb[l])
        xs = xs + gt1 * _rmsnorm(y, norm_mix_post[l])
        h = _rmsnorm(xs, norm_ffn_pre[l]) * (1.0 + sc2) + sh2
        xs = xs + gt2 * _rmsnorm(_channel_mixer(h, l, *ffn_w), norm_ffn_post[l])

    new_win_k = jnp.stack(ctx_new[0], axis=1)
    new_win_v = jnp.stack(ctx_new[1], axis=1)
    new_diff_k = jnp.stack(ctx_new[2], axis=1)
    new_diff_v = jnp.stack(ctx_new[3], axis=1)
    new_mla_ckv = jnp.stack(ctx_new[4], axis=1)
    new_mla_kpe = jnp.stack(ctx_new[5], axis=1)
    new_na_k = jnp.stack(ctx_new[6], axis=1)
    new_na_v = jnp.stack(ctx_new[7], axis=1)
    return (xp, xs, new_win_k, new_win_v, new_diff_k, new_diff_v, new_mla_ckv, new_mla_kpe, new_na_k, new_na_v)


_drawn_inputs = setup_inputs


def setup_inputs(seed=0):
    import zlib

    import numpy as np

    out = dict(_drawn_inputs(seed))
    spreads = {}
    factors = {}
    for name, (base, spread) in spreads.items():
        noise = np.random.default_rng([zlib.crc32(name.encode()), seed]).standard_normal(out[name].shape)
        drawn = base * np.exp(spread * noise) if base else spread * noise
        out[name] = jnp.asarray(drawn.astype(out[name].dtype))
    for name, factor in factors.items():
        out[name] = (out[name] * factor).astype(out[name].dtype)
    return out
```

```python
import math
from contextlib import ExitStack

import numpy as np
import concourse.bass as bass
from concourse import mybir

F32 = mybir.dt.float32
F32R = mybir.dt.float32r
I32 = mybir.dt.int32
ALU = mybir.AluOpType
ACT = mybir.ActivationFunctionType
AX = mybir.AxisListType.X

P = 128
D = 1024
KT = D // P
DEPTH = 2
EPS = 1e-6
GRID_W = 64
HD = 64
NA_COLS = 16
RPB_R, RPB_C = 15, 31
IN_W = 2400
FF = 2816
NE = 8
FE = 3584
QR = 192
UNIT = 2048
NRAW = 6
NSPL = 2
CM = 72
WIN_N = 480
NWIN = IN_W // WIN_N
NFF = FF // 256
NJ = FE // 512
CAP = P

QA, KA, VA, QB, KB, VB, CQ, CKV, KPE, QD, KD, VD = 0, 256, 384, 512, 768, 1024, 1280, 1472, 1600, 1632, 1888, 2144

C_ID, C_UP, C_ONE, C_IOTA, C_ANTI, C_MASK = 0, 128, 256, 384, 512, 640
C_COS64, C_SIN64, C_COS32, C_SIN32, C_REV8, C_SEL, C_NEGH, C_SELB = 768, 832, 896, 928, 960, 968, 970, 972
C_N = C_SELB + 256

KEYS = {"A": 0, "B0": 1, "B1": 2, "D": 3, "C": 5, "rope": 7}
QZ = {"A": 0, "D": 1, "C": 2, "B0": 3, "B1": 4, "rope": 5}
O_COL = {"A": 0, "B0": 256, "B1": 384, "C": 512, "D": 768}

K_WK, K_DK, K_NK, K_CKV, K_KPE, K_N = 0, 128, 384, 640, 768, 800
V_W, V_D, V_N, V_ALL = 0, 128, 384, 640
R_SINK, R_LAM, R_SUB, R_QN, R_KVN, R_N = 0, 4, 132, 196, 388, 516

ITEMS = ["A", "B0", "B1", "D", "C"]
PREP = [["A", "B0", "B1", "D", "C1", "C2", "C3", "C4", "C5"],
        ["A", "B0", "B1", "D", "C1", "C2", "C3", "C4", "C5", "Dc", "BM"]]
SCALE = {"A": HD ** -0.5, "B0": 32 ** -0.5, "B1": 32 ** -0.5, "D": HD ** -0.5, "C": 96 ** -0.5}


def constants():
    c = np.zeros((P, C_N), np.float32)
    i = np.arange(P)
    c[:, C_ID:C_ID + P] = np.eye(P)
    c[:, C_UP:C_UP + P] = i[:, None] < i[None, :]
    c[:, C_ONE:C_ONE + P] = 1.0
    c[:, C_IOTA:C_IOTA + P] = i[None, :]
    c[:, C_ANTI:C_ANTI + P] = (i[:, None] // GRID_W == i[None, :] // GRID_W) & \
        (i[:, None] % GRID_W + i[None, :] % GRID_W == GRID_W - 1)
    qc, kc = i[:, None] % GRID_W, i[None, :] % GRID_W
    start = np.clip(qc - NA_COLS // 2, 0, GRID_W - NA_COLS)
    c[:, C_MASK:C_MASK + P] = np.where((kc >= start) & (kc < start + NA_COLS), 0.0, -1e30)
    for width, cc, sc in ((64, C_COS64, C_SIN64), (32, C_COS32, C_SIN32)):
        h = width // 2
        inv = np.float32(10000.0) ** (-np.arange(0, h, 2, dtype=np.float32) / np.float32(h))
        for half, pos in ((0, i // GRID_W), (1, i % GRID_W)):
            ang = pos.astype(np.float32)[:, None] * inv[None, :]
            o = half * h
            c[:, cc + o:cc + o + h] = np.concatenate([np.cos(ang), np.cos(ang)], 1)
            c[:, sc + o:sc + o + h] = np.concatenate([-np.sin(ang), np.sin(ang)], 1)
    c[:, C_REV8:C_REV8 + 8] = 8 - np.arange(8)
    for s in range(2):
        for r in (s, s + 2, 4):
            c[r, C_SEL + s] = 1.0
            for base in (32, 64):
                c[base + r, C_SELB + s * P:C_SELB + (s + 1) * P] = 1.0
    c[:, C_NEGH] = -0.5
    return c


BASE = [0, 38 + 3 * NFF]
FFN_U = BASE[0] + 38
MOE_U = BASE[1] + 38


def ada_u(l, c):
    return BASE[l] + (2 * c if c < 4 else 10 + 2 * c)


def win_u(l, j):
    return BASE[l] + 8 + 2 * j


def wo_u(l, j):
    return BASE[l] + 34 + 2 * j


def ada_end(l, c):
    return ada_u(l, c) + 2


def win_end(l, j):
    return win_u(l, j) + 2


def y_end(l, which):
    return FFN_U + 3 * NFF if which else wo_u(l, 1) + 2


def bcast_row(src, l, n, parts=P):
    return bass.AP(tensor=src.tensor, offset=l * n, ap=[[0, parts], [1, n]])



def program(nc, ins, outs):
    (x_prompt, x_sample, cwk, cwv, cdk, cdv, cckv, ckpe, cnk, cnv, c_lat, c_ctx, w_ada, b_ada,
     n_mix_pre, n_mix_post, n_ffn_pre, n_ffn_post, w_in, w_o, win_sink, lq1, lk1, lq2, lk2, subln,
     q_norm, kv_norm, wuq_d, wukv_d, rpb, fwg, fwu, fwd, router, mwg, mwu, mwd, consts) = ins
    (y_prompt, y_sample, nwk, nwv, ndk, ndv, nckv, nkpe, nnk, nnv) = outs

    with ExitStack() as ctx:
        def sb(name, shape, dt=F32):
            return ctx.enter_context(nc.sbuf_tensor(name, shape, dt))

        def sem(name):
            return ctx.enter_context(nc.semaphore(name))

        raw = sb("raw", [P, NRAW, UNIT])
        w_hi = sb("w_hi", [P, NSPL, UNIT], F32R)
        w_lo = sb("w_lo", [P, NSPL, UNIT], F32R)
        cst = sb("cst", [P, C_N])
        x = sb("x", [P, 2, D])
        xn = sb("xn", [P, 2, D])
        x_hi = sb("x_hi", [P, 2, D], F32R)
        x_lo = sb("x_lo", [P, 2, D], F32R)
        mrow = sb("mrow", [P, D])
        gpost = sb("gpost", [P, D])
        cond = sb("cond", [P, KT, CM], F32R)
        modc = sb("modc", [P, 4, KT, 2])
        gpre = sb("gpre", [P, 4, KT])
        stat = sb("stat", [P, 144])
        par = sb("par", [P, R_N])
        small = sb("small", [P, 256])
        otmp = sb("otmp", [P, 256])
        sm = sb("sm", [P, 2, 32])
        lam = sb("lam", [P, 8])
        qz = sb("qz", [P, 2, 6, 4, P])
        h_hi = sb("h_hi", [P, 512], F32R)
        h_lo = sb("h_lo", [P, 512], F32R)
        pos = sb("pos", [P, 2, 2, NE + 1])
        comb = sb("comb", [P, 2, NE + 1])
        flag = sb("flag", [P, 1], I32)
        REGION = 11904
        region = sb("region", [P, REGION])
        proj = [region[:, s * IN_W:(s + 1) * IN_W] for s in range(2)]
        o1 = 2 * IN_W
        keys = [region[:, o1 + 1024 * s:o1 + 1024 + 2048 * s] for s in range(2)]
        o2 = o1 + 3072
        v_mla = [region[:, o2 + 256 * s:o2 + 256 + 512 * s] for s in range(2)]
        bm = region[:, o2 + 768:o2 + 1280]
        vcache = region[:, o2 + 1280:o2 + 1280 + V_ALL]
        o3 = o2 + 1280 + V_ALL
        kcache = region[:, o3:o3 + K_N]
        wuq = region[:, o3 + K_N:o3 + K_N + 768]
        wukv = region[:, o3 + K_N + 768:o3 + K_N + 1280]
        probs = region[:, o3:o3 + 2048].rearrange("p (s h k) -> p s h k", s=2, h=4)
        assert o3 + K_N + 1280 <= REGION, o3 + K_N + 1280
        pt_sb = [proj[1][:, QB:QB + 512], proj[1][:, QD:QD + 512]]
        ct = [xn[:, s, 512:1024] for s in range(2)]
        hT = [region[:, D * s:D * (s + 1)] for s in range(2)]
        hrow = [region[:, 2048 + D * s:2048 + D * (s + 1)] for s in range(2)]
        sil = region[:, 4096:4608]
        hid = region[:, 4608:5120]
        y_sb = region[:, 5120:6144]
        acc = [region[:, 6144 + D * s:6144 + D * (s + 1)] for s in range(2)]
        pick = region[:, 8192:8448].rearrange("p (s c) -> p s c", s=2)
        pickw = region[:, 8448:8704].rearrange("p (s c) -> p s c", s=2)
        back = region[:, 8704:8960].rearrange("p (s c) -> p s c", s=2)
        hTn = [region[:, o1 + D * s:o1 + D * (s + 1)] for s in range(2)]
        rt = region[:, 8960:9152].rearrange("p (a b) -> p a b", a=12)
        rtr = region[:, 9152:9216].rearrange("p (k e) -> p k e", k=KT)
        kp4 = [xn[:, 0, 384:512], xn[:, 1, 0:128], xn[:, 1, 128:256]]
        rows_c = region[0:16, 9000:9128]
        rows_s = region[0:16, 9128:9256]
        rows_g = region[0:32, 9256:9384]

        ps = ctx.enter_context(nc.psum_tensor("ps", [P, 8, 512], F32))

        def ident(n=P):
            return cst[0:n, C_ID:C_ID + n]

        def h_of(l, which):
            return hT if which else hTn

        raw_in = [sem(f"raw_in{i}") for i in range(NRAW)]
        hi_done, lo_done, hi_used, used = sem("hi_done"), sem("lo_done"), sem("unit_hi_used"), sem("unit_used")
        in_cst, in_c, in_g = sem("in_cst"), sem("in_c"), sem("in_g")
        in_x = [sem("in_x0"), sem("in_x1")]
        in_rtr = sem("in_rtr")
        in_layer = [sem("in_layer0"), sem("in_layer1")]
        in_brow = [sem("in_brow_c"), sem("in_brow_g1"), sem("in_brow_g2")]
        in_gpost = [sem("in_gpost0"), sem("in_gpost1")]
        qz_zero, cond_silu, init_T, init_cols = sem("qz_zero"), sem("cond_silu"), sem("init_T"), sem("init_cols")
        row_evac, col_mm, col_evac, gate_ready = (sem(n) for n in ("row_evac", "col_mm", "col_evac", "gate_ready"))
        nsq, nrs, nxn, nT, nh, nhi, nlo = (sem(n) for n in ("norm_sq", "norm_rstd", "norm_rows", "norm_T", "norm_h", "norm_hi", "norm_lo"))
        win_evac = [sem("win_evac0"), sem("win_evac1")]
        roped, kp4_ready = sem("roped"), [sem("kp4_ready0"), sem("kp4_ready1")]
        csq, crs = sem("c_sq"), sem("c_rstd")
        cnorm = sem("c_norm")
        m_done = sem("moe_done")
        qr_ready = sem("qr_ready")
        prep_mm = [sem("prep_mm0"), sem("prep_mm1")]
        prep_evac = [sem("prep_evac0"), sem("prep_evac1")]
        scores, sm_bias, probs_ready, pT, pt_evac, o_mm, o_evac = (sem(n) for n in ("scores", "softmax_bias", "probs_ready", "probs_T", "probs_T_evac", "o_mm", "o_evac"))
        sink_d, sink_e = sem("sink_arg"), sem("sink_exp")
        lam_s, lam_e = sem("lam_sums"), sem("lam_exp")
        dsq, drs, o_ready, oT, o_hi, o_lo = (sem(n) for n in ("diff_sq", "diff_rstd", "o_ready", "o_T", "o_hi", "o_lo"))
        psq, prs, gb, gbs, x_upd = (sem(n) for n in ("post_sq", "post_rstd", "gate_bcast", "gate_bcast_sbuf", "x_updated"))
        f_sil, f_h, f_T, f_hi, f_lo = (sem(n) for n in ("ffn_silu", "ffn_h", "ffn_hT", "ffn_h_hi", "ffn_h_lo"))
        r_mm, r_rowT, r_row, r_diff, r_exp, r_mask, r_pos, r_ready = (sem(n) for n in ("rt_logits", "rt_rows", "rt_rows_evac", "rt_diff", "rt_exp", "rt_mask", "rt_pos", "rt_ready"))
        m_pick, m_gath, m_xhi, m_xlo, m_pw, m_bT, m_back = (sem(n) for n in ("moe_pick", "moe_gather", "moe_x_hi", "moe_x_lo", "moe_pick_w", "moe_back_T", "moe_back"))
        m_sil, m_h, m_T, m_hi, m_lo = (sem(n) for n in ("moe_silu", "moe_h", "moe_hT", "moe_h_hi", "moe_h_lo"))
        m_y0, m_y1, m_c, m_acc = (sem(n) for n in ("moe_y_half0", "moe_y_half1", "moe_comb", "moe_acc"))
        out_ctx = [sem("out_ctx0"), sem("out_ctx1")]
        out_x = sem("out_x")
        pool_step, act_step, dve_step = sem("pool_step"), sem("act_step"), sem("dve_step")
        NOUT = 8 * 16
        N_LAYER = (6 + 2 + 6 + 8 + 4) * 16

        def col_idx(l, k):
            return 4 * l + (0, 1, None, 2, 3)[k]

        def np_(s):
            return len(PREP[s])

        def nk_of(s):
            return P * (1 + s)

        def wait_sum(eng, s, t, c):
            eng.wait_ge(s, t + c)

        def prep_copies(s, step, b):
            nk, k = nk_of(s), keys[s]

            def halves(i, src):
                return [(qz[64 * g:64 * g + 64, s, i, g:4:2, :],
                         ps[64 * g:64 * g + 64, b, src:src + 256].rearrange("p (r q) -> p r q", r=2)) for g in range(2)]

            def quarters(i):
                return [(qz[32 * j:32 * j + 32, s, i, j, :], ps[32 * j:32 * j + 32, b, 0:P]) for j in range(4)]

            def blocks(n, count=1):
                return k[:, KEYS[n] * nk:(KEYS[n] + count) * nk]

            def pairs(n, src, nks):
                return (blocks(n, 2).rearrange("p (r k) -> p r k", r=2)[:, :, nks:nks + src.shape[2]], src)

            if step == "A":
                return halves(QZ["A"], 0) + [(blocks("A"), ps[:, b, 256:256 + nk])]
            if step in ("B0", "B1"):
                return quarters(QZ[step]) + [(blocks(step), ps[:, b, P:P + nk])]
            if step == "D":
                return halves(QZ["D"], 0) + [pairs("D", ps[:, b, 256:512].rearrange("p (r k) -> p r k", r=2), 0)]
            if step == "Dc":
                return [pairs("D", ps[:, b, 0:256].rearrange("p (r k) -> p r k", r=2), P)]
            if step == "C1":
                return [(ct[s][0:96, 0:256], ps[0:96, b, 0:256]), (ct[s][:, 256:256 + nk], ps[:, b, 256:256 + nk])]
            if step == "C2":
                return [(small[:, P * s:P * s + P], ps[:, b, 256:384])] + halves(QZ["C"], 0)
            if step == "C3":
                return [pairs("C", ps[:, b, :].rearrange("p (r k) -> p r k", r=2)[:, :, 0:nk], 0)]
            if step == "C4":
                return [(v_mla[s][:, 0:2 * nk], ps[:, b, 0:2 * nk])]
            return quarters(QZ["rope"]) + [(blocks("rope"), ps[:, b, P:P + nk])]

        def proj_copies(s, j):
            src = ps[:, 2 + 2 * (j % 2) + s, :]
            o = WIN_N * j
            if j:
                return [(proj[s][:, o:o + WIN_N], src[:, 0:WIN_N])]
            return [(proj[s][:, 0:256].rearrange("p (r g d) -> p r g d", r=2, g=2),
                     src[:, 0:256].rearrange("p (g r d) -> p r g d", r=2, g=2)),
                    (proj[s][:, 256:WIN_N], src[:, 256:WIN_N])]

        def score_view(s):
            if s == 0:
                return ps[:, 2, :].rearrange("p (h k) -> p h k", h=4)
            return ps[:, 4:6, :].rearrange("p a (b k) -> p (a b) k", b=2)

        def width(u):
            return 4 * WIN_N if any(win_u(l, 0) <= u < win_u(l, NWIN) for l in range(DEPTH)) else UNIT

        def split_hi(c, n):
            return w_hi[:, c % NSPL, n]

        def split_lo(c, n):
            return w_lo[:, c % NSPL, n]

        block = ctx.enter_context(nc.Block())

        @block.sync
        def _(sp):
            def load(u, slot, dst, src):
                if not (isinstance(u, int) and u < NRAW):
                    sp.wait_ge(lo_done, u - NRAW + 1)
                sp.dma_start(dst, src).then_inc(raw_in[slot], 16)

            def load_k(u, src, rows0, cols, col0=0):
                dst = raw[:, u % NRAW, 0:4 * cols].rearrange("p (k n) -> p k n", k=4)
                load(u, u % NRAW, dst, src[rows0:rows0 + 512, col0:col0 + cols].rearrange("(k p) n -> p k n", p=P))

            def ada(l, c):
                for h in range(2):
                    load_k(ada_u(l, c) + h, w_ada[l], 512 * h, 512, 512 * c)

            for l in range(DEPTH):
                for c in range(4):
                    ada(l, c)
                for j in range(NWIN):
                    for h in range(2):
                        load_k(win_u(l, j) + h, w_in[l], 512 * h, WIN_N, WIN_N * j)
                for c in range(4, 12):
                    ada(l, c)
                for j in range(2):
                    for h in range(2):
                        load_k(wo_u(l, j) + h, w_o[l], 512 * h, 512, 512 * j)
                if l == 0:
                    def ffn_gu(u, slot, w, f):
                        load(u, slot, raw[:, slot, :].rearrange("p (k n) -> p k n", k=KT),
                             w[0, :, bass.ds(256 * f, 256)].rearrange("(k p) n -> p k n", p=P))

                    def ffn_d(u, slot, f):
                        load(u, slot, raw[:, slot, :].rearrange("p (t n) -> p t n", t=2),
                             fwd[0, bass.ds(256 * f, 256), :].rearrange("(t p) n -> p t n", p=P))

                    ffn_gu(FFN_U, FFN_U % NRAW, fwg, 0)
                    ffn_gu(FFN_U + 1, (FFN_U + 1) % NRAW, fwu, 0)
                    with sp.Fori(0, (NFF - 1) // 2) as i:
                        for k in range(2):
                            u, s0 = 6 * i + (FFN_U + 2 + 3 * k), FFN_U + 2 + 3 * k
                            ffn_gu(u, s0 % NRAW, fwg, 2 * i + (k + 1))
                            ffn_gu(u + 1, (s0 + 1) % NRAW, fwu, 2 * i + (k + 1))
                            ffn_d(u + 2, (s0 + 2) % NRAW, 2 * i + k)
                    ffn_d(FFN_U + 3 * NFF - 1, (FFN_U + 3 * NFF - 1) % NRAW, NFF - 1)

            def moe_gu(u, slot, w, e, j, h):
                load(u, slot, raw[:, slot, :].rearrange("p (k n) -> p k n", k=4),
                     w[0, bass.ds(e, 1), 512 * h:512 * h + 512, bass.ds(512 * j, 512)]
                     .rearrange("a (k p) n -> p (a k) n", p=P))

            def moe_d(u, slot, e, j, h):
                load(u, slot, raw[:, slot, :].rearrange("p (t n) -> p t n", t=2),
                     mwd[0, bass.ds(e, 1), bass.ds(512 * j + 256 * h, 256), :]
                     .rearrange("a (t p) n -> p (a t) n", p=P))

            def moe_pass(p):
                b = MOE_U + p * 42 * NE
                with sp.Fori(0, NE) as e:
                    for k, w in ((0, mwg), (2, mwu)):
                        for h in range(2):
                            moe_gu(42 * e + (b + k + h), (b + k + h) % NRAW, w, e, 0, h)
                    with sp.Fori(1, NJ) as j:
                        for k, w in ((0, mwg), (2, mwu)):
                            for h in range(2):
                                moe_gu(42 * e + 6 * j + (b - 2 + k + h), (b + 4 + k + h) % NRAW, w, e, j, h)
                        for h in range(2):
                            moe_d(42 * e + 6 * j + (b + 2 + h), (b + 8 + h) % NRAW, e, j - 1, h)
                    for h in range(2):
                        moe_d(42 * e + (b + 40 + h), (b + 40 + h) % NRAW, e, NJ - 1, h)

            moe_pass(0)
            sp.wait_ge(r_ready, 1)
            n = sp.value_load(flag[0:1, 0:1], min_val=0, max_val=2 * P)
            with sp.If(n > CAP):
                moe_pass(1)
            for s, y in ((0, y_prompt), (1, y_sample)):
                sp.wait_ge(x_upd, 7 + s)
                sp.dma_start(y[0], x[:, s, :]).then_inc(out_x, 16)
            sp.wait_ge(out_x, 32)
            for l in range(DEPTH):
                sp.wait_ge(out_ctx[l], NOUT)

        @block.gpsimd
        def _(pool):
            steps = [0]

            def link(i):
                steps[0] += 1
                i.then_inc(pool_step, 1)
                pool.wait_ge(pool_step, steps[0])

            pool.dma_start(rows_c[0:8, :], c_ctx.rearrange("(k n) -> k n", k=KT)).then_inc(in_c, 16)
            pool.dma_start(rows_c[8:16, :], c_lat[0].rearrange("(k n) -> k n", k=KT)).then_inc(in_c, 16)
            pool.dma_start(cst[:, :], consts).then_inc(in_cst, 16)
            pool.dma_start(x[:, 0, :], x_prompt[0]).then_inc(in_x[0], 16)
            pool.dma_start(x[:, 1, :], x_sample[0]).then_inc(in_x[1], 16)
            for i, v in enumerate((n_mix_pre, n_ffn_pre)):
                pool.dma_start(rows_g[16 * i:16 * i + 16, :], v.rearrange("l (k n) -> (l k) n", k=KT)).then_inc(in_g, 16)

            def brow(l, k):
                kind = {2: 1, 5: 2}.get(k, 0)
                if kind == 0 and col_idx(l, k) > 0:
                    pool.wait_ge(col_mm, col_idx(l, k))
                if kind and l:
                    pool.wait_ge(gb, 4 * (l - 1) + 2 * kind)
                r = 32 * kind + 4
                pool.dma_start(mrow[r:r + 1, :], b_ada[l:l + 1, D * k:D * k + D]).then_inc(in_brow[kind], 16)

            def rstd(dst, tmp, ssq, width, done):
                link(pool.tensor_scalar(tmp, ssq, 1.0 / width, EPS, ALU.mult, ALU.add))
                n = tmp.shape[-1]
                i = pool.tensor_tensor(dst, tmp, cst[:, C_NEGH:C_NEGH + 1].to_broadcast([P, n]), ALU.pow)
                if done is not None:
                    i.then_inc(done, 1)
                return i

            def norm(l, which):
                for s in range(2):
                    q = 4 * l + 2 * which + s
                    pool.wait_ge(nsq, q + 1)
                    rstd(stat[:, 3 * q + 2:3 * q + 3], stat[:, 3 * q + 1:3 * q + 2], stat[:, 3 * q:3 * q + 1], D, nrs)

            def post(l, which):
                for s in range(2):
                    q = 4 * l + 2 * which + s
                    pool.wait_ge(psq, q + 1)
                    o = 24 + 3 * q
                    rstd(stat[:, o + 2:o + 3], stat[:, o + 1:o + 2], stat[:, o:o + 1], D, prs)

            def layer_loads(l):
                q = in_layer[l]
                if l:
                    pool.wait_ge(o_ready, 2)
                    pool.wait_ge(gate_ready, 2)
                    pool.wait_ge(pt_evac, 10)
                else:
                    pool.wait_ge(init_cols, 1)
                for dst, src in ((kcache[:, K_WK:K_WK + 128], cwk), (kcache[:, K_DK:K_DK + 256], cdk),
                                 (kcache[:, K_NK:K_NK + 256], cnk), (vcache[:, V_W:V_W + 128], cwv),
                                 (vcache[:, V_D:V_D + 256], cdv), (vcache[:, V_N:V_N + 256], cnv)):
                    pool.dma_start(dst.rearrange("p (h d) -> p h d", d=HD),
                                   src[0, l].rearrange("h t d -> t h d")).then_inc(q, 16)
                pool.dma_start(kcache[:, K_CKV:K_CKV + 128], cckv[0, l]).then_inc(q, 16)
                pool.dma_start(kcache[:, K_KPE:K_KPE + 32], ckpe[0, l]).then_inc(q, 16)
                for i in range(2):
                    src = wuq_d[l, 96 * i:96 * i + 96, :].rearrange("p (h d) -> p h d", h=4)
                    o = 384 * i
                    pool.dma_start(wuq[0:96, o:o + 256].rearrange("p (h d) -> p h d", h=4), src[:, :, 0:HD]).then_inc(q, 16)
                    pool.dma_start(wuq[0:96, o + 256:o + 384].rearrange("p (h d) -> p h d", h=4), src[:, :, HD:96]).then_inc(q, 16)
                src = wukv_d[l].rearrange("p (h d) -> p h d", h=4)
                pool.dma_start(wukv[:, 0:256].rearrange("p (h d) -> p h d", h=4), src[:, :, 0:HD]).then_inc(q, 16)
                pool.dma_start(wukv[:, 256:512].rearrange("p (h d) -> p h d", h=4), src[:, :, HD:P]).then_inc(q, 16)
                for o, n, v in ((R_SINK, 4, win_sink), (R_LAM, 32, lq1), (R_LAM + 32, 32, lk1), (R_LAM + 64, 32, lq2),
                                (R_LAM + 96, 32, lk2), (R_SUB, 64, subln), (R_QN, QR, q_norm), (R_KVN, P, kv_norm)):
                    pool.dma_start(par[:, o:o + n], bcast_row(v, l, n)).then_inc(q, 16)
                for qr in range(2):
                    for kr in range(2):
                        first = (l * 4 * RPB_R + kr - qr + 7) * RPB_C - (GRID_W - 1) + NA_COLS - 1
                        pool.dma_start(bm[64 * qr:64 * qr + 64, :].rearrange("p (h k) -> p h k", h=4)[:, :, 64 * kr:64 * kr + 64],
                                       bass.AP(tensor=rpb.tensor, offset=first,
                                               ap=[[1, 64], [RPB_R * RPB_C, 4], [1, 64]])).then_inc(q, 16)
                for i, v in ((1, n_mix_post), (2, n_ffn_post)):
                    pool.dma_start(gpost[32 * i:32 * i + 5, :], bcast_row(v, l, D, 5)).then_inc(in_gpost[l], 16)

            def context_outputs(l):
                pool.wait_ge(win_evac[0], NWIN * (l + 1))
                for o, n, dst in ((KA, 2, nwk), (VA, 2, nwv), (KB, 4, ndk), (VB, 4, ndv), (KD, 4, nnk), (VD, 4, nnv)):
                    pool.dma_start(dst[0, l].rearrange("h t d -> t h d"),
                                   proj[0][:, o:o + n * HD].rearrange("p (h d) -> p h d", d=HD)).then_inc(out_ctx[l], 16)
                pool.dma_start(nkpe[0, l], proj[0][:, KPE:KPE + 32]).then_inc(out_ctx[l], 16)
                pool.wait_ge(cnorm, 2 * l + 1)
                pool.dma_start(nckv[0, l], proj[0][:, CKV:CKV + P]).then_inc(out_ctx[l], 16)

            for l in range(DEPTH):
                if l == 0:
                    for k in (0, 2, 5):
                        brow(0, k)
                    pool.memset(qz[:, :, :, :, :], 0.0).then_inc(qz_zero, 1)
                    norm(0, 0)
                    layer_loads(0)
                brow(l, 1)
                if l:
                    norm(l, 0)
                for s in range(2):
                    n = 2 * l + s
                    pool.wait_ge(csq, n + 1)
                    o = 48 + 6 * n
                    link(pool.tensor_scalar(stat[:, o + 2:o + 3], stat[:, o:o + 1], 1.0 / QR, EPS, ALU.mult, ALU.add))
                    link(pool.tensor_scalar(stat[:, o + 3:o + 4], stat[:, o + 1:o + 2], 1.0 / P, EPS, ALU.mult, ALU.add))
                    pool.tensor_tensor(stat[:, o + 4:o + 6], stat[:, o + 2:o + 4],
                                       cst[:, C_NEGH:C_NEGH + 1].to_broadcast([P, 2]), ALU.pow).then_inc(crs, 1)
                context_outputs(l)
                brow(l, 3)
                brow(l, 4)
                for s in range(2):
                    n = 2 * l + s
                    pool.wait_ge(dsq, n + 1)
                    o = 72 + 12 * n
                    rstd(stat[:, o + 8:o + 12], stat[:, o + 4:o + 8], stat[:, o:o + 4], HD, drs)
                post(l, 0)
                norm(l, 1)
                if l == 0:
                    brow(1, 0)
                    brow(1, 2)
                    layer_loads(1)
                    post(0, 1)
                    brow(1, 5)
            pool.wait_ge(x_upd, 6)
            pool.dma_start(rtr, router[0].rearrange("(k p) e -> p k e", p=P)).then_inc(in_rtr, 16)
            post(1, 1)


        @block.scalar
        def _(act):
            split = [0]

            def hi(t, c):
                act.wait_ge(raw_in[c % NRAW], 16 * t + 16 * (c // NRAW + 1))
                if c >= NSPL:
                    act.wait_ge(hi_used, 6 * t + (c - NSPL + 1))
                    act.wait_ge(lo_done, 6 * t + (c - NSPL + 1))
                act.activation(split_hi(c, slice(0, width(c))), raw[:, c % NRAW, 0:width(c)], ACT.Copy).then_inc(hi_done, 1)

            def split_to(end):
                for u in range(split[0], end):
                    hi(0, u)
                split[0] = max(split[0], end)

            steps = [0]

            def link(i):
                steps[0] += 1
                i.then_inc(act_step, 1)
                act.wait_ge(act_step, steps[0])

            act.wait_ge(in_c, 32)
            act.activation(rows_s, rows_c, ACT.Silu).then_inc(cond_silu, 1)

            def ada(l, c):
                k = c // 2
                split_to(ada_u(l, c) + 3)
                kind = {2: 1, 5: 2}.get(k, 0)
                if kind == 0 and c % 2 == 0 and col_idx(l, k) > 0:
                    act.wait_ge(col_mm, col_idx(l, k))
                if kind and c % 2 == 0 and l:
                    act.wait_ge(gb, 4 * (l - 1) + 2 * kind)
                act.wait_ge(used, ada_end(l, c))
                act.activation(mrow[32 * kind:32 * kind + 4, 512 * (c % 2):512 * (c % 2) + 512], ps[0:4, 7, :],
                               ACT.Copy).then_inc(row_evac, 1)

            def norm_rows(l, which):
                for s in range(2):
                    q = 4 * l + 2 * which + s
                    if q < 2:
                        act.wait_ge(in_x[s], 16)
                    else:
                        act.wait_ge(x_upd, q - 1)
                    act.activation(xn[:, s, :], x[:, s, :], ACT.Square, accum_out=stat[:, 3 * q:3 * q + 1]).then_inc(nsq, 1)
                for s in range(2):
                    q = 4 * l + 2 * which + s
                    act.wait_ge(nrs, q + 1)
                    act.activation(xn[:, s, :], x[:, s, :], ACT.Copy, scale=stat[:, 3 * q + 2:3 * q + 3]).then_inc(nxn, 1)

            def norm_hi(l, which):
                for s in range(2):
                    act.wait_ge(nh, 4 * l + 2 * which + s + 1)
                    act.activation(x_hi[:, s, :], h_of(l, which)[s], ACT.Copy).then_inc(nhi, 1)

            def prep(l, k):
                act.wait_ge(prep_mm[0], np_(0) * l + k + 1)
                if l == 0 and k == 0:
                    act.wait_ge(qz_zero, 1)
                for dst, src in prep_copies(0, PREP[0][k], 2 * (k % 3)):
                    last = act.activation(dst, src, ACT.Copy)
                last.then_inc(prep_evac[0], 1)

            def exps(l, i):
                it, s = ITEMS[i // 2], i % 2
                act.wait_ge(sm_bias, 10 * l + i + 1)
                nk = nk_of(s)
                biased = it == "D" and s == 1
                for h in range(4):
                    src = probs[:, s, h, 0:nk] if biased else score_view(s)[:, h, :]
                    last = act.activation(probs[:, s, h, 0:nk], src, ACT.Exp, bias=sm[:, s, 4 + h:5 + h],
                                          scale=1.0 if biased else SCALE[it], accum_out=sm[:, s, 8 + h:9 + h])
                last.then_inc(probs_ready, 1)
                if it == "A":
                    act.wait_ge(sink_d, 2 * l + s + 1)
                    act.activation(sm[:, s, 16:20], sm[:, s, 12:16], ACT.Exp).then_inc(sink_e, 1)

            def post_sq(l, which):
                for s in range(2):
                    q = 4 * l + 2 * which + s
                    if q < 6:
                        act.wait_ge(used, y_end(l, which))
                        src, dst = ps[:, 2 + 2 * s:4 + 2 * s, :], xn[:, s, :].rearrange("p (a b) -> p a b", a=2)
                    else:
                        src, dst = acc[s], xn[:, s, :]
                    act.activation(dst, src, ACT.Square, accum_out=stat[:, 24 + 3 * q:25 + 3 * q]).then_inc(psq, 1)
                for s in range(2):
                    act.wait_ge(psq, 4 * l + 2 * which + s + 1)
                    act.wait_ge(gb, 4 * l + 2 * which + s + 1)
                    act.activation(xn[:, s, :].rearrange("p (a b) -> p a b", a=2), ps[:, 6:8, :], ACT.Copy).then_inc(gbs, 1)

            def ffn():
                split_to(FFN_U + 2)

                def silu(gu_end):
                    act.wait_ge(used, gu_end)
                    act.activation(sil.rearrange("p (s n) -> p s n", s=2), ps[:, 6:8, 0:256], ACT.Silu).then_inc(f_sil, 1)

                def h_round(f):
                    act.wait_ge(f_T, f + 1)
                    act.activation(h_hi[:, :].rearrange("p (s n) -> p s n", s=2), ps[:, 0:2, 0:256], ACT.Copy).then_inc(f_hi, 1)

                silu(FFN_U + 2)
                with act.Fori(0, (NFF - 1) // 2) as i:
                    for k in range(2):
                        c = FFN_U + 2 + 3 * k
                        hi(i, c)
                        hi(i, c + 1)
                        h_round(2 * i + k)
                        hi(i, c + 2)
                        silu(6 * i + (c + 2))
                split[0] = FFN_U + 2 + 3 * (NFF - 1)
                split_to(FFN_U + 3 * NFF)
                h_round(NFF - 1)

            def route():
                act.wait_ge(r_rowT, 1)
                act.activation(hrow[0].rearrange("p (a b) -> p a b", a=2), ps[:, 0:2, :], ACT.Copy).then_inc(r_row, 1)
                act.wait_ge(r_diff, 1)
                act.activation(rt[:, 11, 8:10], rt[:, 11, 6:8], ACT.Exp).then_inc(r_exp, 1)
                act.activation(rt[:, 9, 0:1], rt[:, 11, 6:7], ACT.Copy).then_inc(m_sil, 1)

            def gathered_hi(n):
                act.wait_ge(m_gath, n + 1)
                act.activation(x_hi[:, 0, :].rearrange("p (a b) -> p a b", a=2), ps[:, 4:6, :], ACT.Copy).then_inc(m_xhi, 1)

            def moe(p):
                b = MOE_U + 42 * NE * p

                def silu(gu_end):
                    act.wait_ge(used, gu_end)
                    act.activation(sil, ps[:, 6, :], ACT.Silu).then_inc(m_sil, 1)

                def h_round(n):
                    act.wait_ge(m_T, n + 1)
                    act.activation(h_hi[:, :], ps[:, 0, :], ACT.Copy).then_inc(m_hi, 1)

                def y_half(e):
                    act.wait_ge(used, 42 * e + (b + 42))
                    act.activation(y_sb[:, 0:512], ps[:, 2, :], ACT.Copy).then_inc(m_y0, 1)

                def expert(e, first):
                    n0 = 7 * e + 56 * p
                    hi(7 * e, b)
                    hi(7 * e, b + 1)
                    if not first:
                        y_half(e - 1)
                    for k in range(2, 6):
                        hi(7 * e, b + k)
                    silu(42 * e + (b + 4))
                    hi(7 * e, b + 6)
                    act.wait_ge(m_bT, e + (8 * p + 1))
                    if not first:
                        act.wait_ge(m_c, 2 * e + 16 * p)
                    elif p:
                        act.wait_ge(m_c, 16 * p)
                    act.activation(back, ps[:, 1, 0:256].rearrange("p (s c) -> p s c", s=2), ACT.Copy).then_inc(m_back, 1)
                    h_round(n0)
                    for k in range(3, 6):
                        hi(7 * e + 1, b - 2 + k)
                    silu(42 * e + (b + 8))
                    with act.Fori(2, NJ) as j:
                        for k in range(3):
                            hi(7 * e + j, b - 2 + k)
                        h_round(n0 + j - 1)
                        for k in range(3, 6):
                            hi(7 * e + j, b - 2 + k)
                        silu(42 * e + 6 * j + (b + 2))
                    hi(7 * e, b + 40)
                    hi(7 * e, b + 41)
                    h_round(n0 + (NJ - 1))
                    gathered_hi(e + (9 * p + 1))

                gathered_hi(9 * p)
                expert(0, True)
                with act.Fori(1, NE) as e:
                    expert(e, False)
                y_half(NE - 1)

            for l in range(DEPTH):
                if l == 0:
                    norm_rows(0, 0)
                for c in range(4):
                    ada(l, c)
                if l == 1:
                    norm_rows(1, 0)
                norm_hi(l, 0)
                if l:
                    act.wait_ge(out_ctx[l - 1], NOUT)
                for j in range(NWIN):
                    split_to(win_u(l, j) + 3)
                    act.wait_ge(used, win_end(l, j))
                    for dst, src in proj_copies(0, j):
                        last = act.activation(dst, src, ACT.Copy)
                    last.then_inc(win_evac[0], 1)
                act.wait_ge(win_evac[0], NWIN * (l + 1))
                for s in range(2):
                    if s:
                        act.wait_ge(win_evac[1], NWIN * (l + 1))
                    o, r = 192 * s, 48 + 6 * (2 * l + s)
                    act.activation(xn[:, 0, o:o + QR], proj[s][:, CQ:CQ + QR], ACT.Square, accum_out=stat[:, r:r + 1])
                    act.activation(otmp[:, 128 * s:128 * s + P], proj[s][:, CKV:CKV + P], ACT.Square,
                                   accum_out=stat[:, r + 1:r + 2]).then_inc(csq, 1)
                    if s == 0:
                        act.activation(kp4[0].rearrange("p (h d) -> p h d", h=4),
                                       proj[0][:, KPE:KPE + 32].unsqueeze(1).to_broadcast([P, 4, 32]), ACT.Copy).then_inc(kp4_ready[0], 1)
                act.wait_ge(lam_s, l + 1)
                act.activation(lam[:, 2:4], lam[:, 0:2], ACT.Exp).then_inc(lam_e, 1)
                for k in range(np_(0)):
                    prep(l, k)
                    if k == 4:
                        ada(l, 4)
                ada(l, 5)
                exps(l, 0)
                for i in range(10):
                    if i + 1 < 10:
                        exps(l, i + 1)
                    if i < 6:
                        ada(l, 6 + i)
                for s in range(2):
                    act.wait_ge(oT, 2 * l + s + 1)
                    act.activation(x_hi[:, s, :].rearrange("p (a b) -> p a b", a=2), ps[:, 6 * s:6 * s + 2, :],
                                   ACT.Copy).then_inc(o_hi, 1)
                split_to(wo_u(l, 2))
                post_sq(l, 0)
                norm_rows(l, 1)
                if l == 0:
                    norm_hi(l, 1)
                    ffn()
                    post_sq(0, 1)

            route()
            moe(0)
            act.wait_ge(r_ready, 1)
            n = act.value_load(flag[0:1, 0:1], min_val=0, max_val=2 * P)
            with act.If(n > CAP):
                moe(1)
            act.wait_ge(m_done, 1)
            post_sq(1, 1)

        @block.vector
        def _(dve):
            steps, split = [0], [0]

            def link(i):
                steps[0] += 1
                i.then_inc(dve_step, 1)
                dve.wait_ge(dve_step, steps[0])

            def lo(t, c):
                dve.wait_ge(hi_done, 6 * t + (c + 1))
                if c >= NSPL:
                    dve.wait_ge(used, 6 * t + (c - NSPL + 1))
                n = slice(0, width(c))
                dve.tensor_sub(split_lo(c, n), raw[:, c % NRAW, n], split_hi(c, n)).then_inc(lo_done, 1)

            def split_to(end):
                for u in range(split[0], end):
                    lo(0, u)
                split[0] = max(split[0], end)

            def b2(v, n):
                return v.unsqueeze(2).to_broadcast([P, v.shape[1], n])

            dve.memset(cond[:, :, :].bitcast(F32), 0.0).then_inc(dve_step, 1)
            steps[0] += 1
            dve.wait_ge(dve_step, steps[0])
            dve.wait_ge(init_T, 1)
            cT = ps[:, 7, 0:16].rearrange("p (s k) -> p k s", s=2)
            link(dve.tensor_copy(cond[:, :, 0:2], cT))
            dve.tensor_sub(cond[:, :, 2:4], cT, cond[:, :, 0:2])
            dve.tensor_copy(gpre[:, :, :], ps[:, 7, 16:48].rearrange("p (a k) -> p a k", k=KT)).then_inc(init_cols, 1)

            def ada(l, c):
                k = c // 2
                split_to(ada_u(l, c) + 3)
                if c % 2 == 0:
                    return
                if k in (2, 5):
                    r, i = (32, 1) if k == 2 else (64, 2)
                    dve.wait_ge(row_evac, 12 * l + c + 1)
                    dve.wait_ge(in_brow[i], 16 * (l + 1))
                    dve.wait_ge(in_gpost[l], 32)
                    dve.tensor_mul(mrow[r:r + 5, :], mrow[r:r + 5, :], gpost[r:r + 5, :]).then_inc(gate_ready, 1)
                    return
                n = col_idx(l, k)
                dve.wait_ge(col_mm, n + 1)
                i = (0, 1, None, 2, 3)[k]
                src = ps[:, 6, 0:16].rearrange("p (k s) -> p k s", s=2)
                if i % 2 == 0:
                    dve.tensor_copy(modc[:, i, :, :], src).then_inc(col_evac, 1)
                else:
                    g = gpre[:, 2 * (i // 2) + l, :]
                    dve.scalar_tensor_tensor(out=modc[:, i, :, :], in0=src, scalar=1.0, in1=b2(g, 2),
                                             op0=ALU.add, op1=ALU.mult).then_inc(col_evac, 1)
                dve.wait_ge(col_evac, n + 1)

            def norm_cols(l, which):
                for s in range(2):
                    q = 4 * l + 2 * which + s
                    h = h_of(l, which)[s].rearrange("p (k t) -> p k t", k=KT)
                    dve.wait_ge(nT, q + 1)
                    link(dve.tensor_tensor(h, ps[:, 2 * s:2 * s + 2, :].rearrange("p a (b t) -> p (a b) t", t=P),
                                           b2(modc[:, 2 * which + 1, :, s], P), ALU.mult))
                    dve.tensor_tensor(h, h, b2(modc[:, 2 * which, :, s], P), ALU.add).then_inc(nh, 1)
                if (l, which) == (1, 1):
                    return
                for s in range(2):
                    dve.wait_ge(nhi, 4 * l + 2 * which + s + 1)
                    dve.tensor_sub(x_lo[:, s, :], h_of(l, which)[s], x_hi[:, s, :]).then_inc(nlo, 1)

            def rope(v, g, w):
                cc, sc = (C_COS64, C_SIN64) if w == 64 else (C_COS32, C_SIN32)
                n = g * w
                t1, t2 = xn[:, 1, 0:n], xn[:, 1, 512:512 + n]
                cos = cst[:, cc:cc + w].unsqueeze(1).to_broadcast([P, g, w])
                sin = cst[:, sc:sc + w].rearrange("p (a b m) -> p a b m", a=2, b=2)
                v4 = v.rearrange("p (g a b m) -> p g a b m", g=g, a=2, b=2)
                t4 = t2.rearrange("p (g a b m) -> p g a b m", g=g, a=2, b=2)
                for a in range(2):
                    for h in range(2):
                        dve.tensor_tensor(t4[:, :, a, h, :], v4[:, :, a, 1 - h, :],
                                          sin[:, a, h, :].unsqueeze(1).to_broadcast([P, g, w // 4]), ALU.mult)
                link(dve.tensor_tensor(t1.rearrange("p (g w) -> p g w", g=g), v.rearrange("p (g w) -> p g w", g=g), cos, ALU.mult))
                return dve.tensor_tensor(v, t1, t2, ALU.add)

            def prep(l, k):
                step, b = PREP[1][k], 2 * (k % 3) + 1
                dve.wait_ge(prep_mm[1], np_(1) * l + k + 1)
                if l == 0 and k == 0:
                    dve.wait_ge(qz_zero, 1)
                if step == "BM":
                    mask = cst[:, C_MASK:C_MASK + P].unsqueeze(1).to_broadcast([P, 4, P])
                    dve.tensor_tensor(bm.rearrange("p (h k) -> p h k", h=4), ps[:, b, :].rearrange("p (h k) -> p h k", h=4),
                                      mask, ALU.add).then_inc(prep_evac[1], 1)
                    return
                for dst, src in prep_copies(1, step, b):
                    last = dve.tensor_copy(dst, src)
                last.then_inc(prep_evac[1], 1)
                if step == "C2":
                    dve.wait_ge(prep_evac[1], np_(1) * l + k + 1)
                    rope_small(small[:, P:2 * P]).then_inc(qr_ready, 1)

            def rope_small(v):
                t1, t2 = otmp[:, 0:P], otmp[:, P:2 * P]
                sin = cst[:, C_SIN32:C_SIN32 + 32].rearrange("p (a b m) -> p a b m", a=2, b=2)
                v4 = v.rearrange("p (g a b m) -> p g a b m", g=4, a=2, b=2)
                t4 = t2.rearrange("p (g a b m) -> p g a b m", g=4, a=2, b=2)
                for a in range(2):
                    for h in range(2):
                        dve.tensor_tensor(t4[:, :, a, h, :], v4[:, :, a, 1 - h, :],
                                          sin[:, a, h, :].unsqueeze(1).to_broadcast([P, 4, 8]), ALU.mult)
                link(dve.tensor_tensor(t1.rearrange("p (g w) -> p g w", g=4), v.rearrange("p (g w) -> p g w", g=4),
                                       cst[:, C_COS32:C_COS32 + 32].unsqueeze(1).to_broadcast([P, 4, 32]), ALU.mult))
                return dve.tensor_tensor(v, t1, t2, ALU.add)

            def soft_pre(l, i):
                it, s = ITEMS[i // 2], i % 2
                sc = SCALE[it]
                v = score_view(s)
                dve.wait_ge(scores, 10 * l + i + 1)
                mx, nb = sm[:, s, 0:4], sm[:, s, 4:8]
                if it == "D" and s == 1:
                    pv = probs[:, 1, :, :]
                    dve.scalar_tensor_tensor(out=pv[:, :, 0:P], in0=v[:, :, 0:P], scalar=sc,
                                             in1=bm.rearrange("p (h k) -> p h k", h=4), op0=ALU.mult, op1=ALU.add)
                    link(dve.tensor_scalar(pv[:, :, P:2 * P], v[:, :, P:2 * P], sc, None, ALU.mult))
                    link(dve.tensor_reduce(mx, pv, AX, ALU.max))
                    dve.tensor_scalar(nb, mx, -1.0, None, ALU.mult).then_inc(sm_bias, 1)
                    return
                link(dve.tensor_reduce(mx, v, AX, ALU.max))
                if it != "A":
                    dve.tensor_scalar(nb, mx, -sc, None, ALU.mult).then_inc(sm_bias, 1)
                    return
                sink = par[:, R_SINK:R_SINK + 4]
                link(dve.scalar_tensor_tensor(out=sm[:, s, 24:28], in0=mx, scalar=sc, in1=sink, op0=ALU.mult, op1=ALU.max))
                dve.tensor_scalar(nb, sm[:, s, 24:28], -1.0, None, ALU.mult).then_inc(sm_bias, 1)
                dve.tensor_sub(sm[:, s, 12:16], sink, sm[:, s, 24:28]).then_inc(sink_d, 1)

            def soft_T(l, i):
                s = i % 2
                dve.wait_ge(pT, 10 * l + i + 1)
                for kb in range(1 + s):
                    last = dve.tensor_copy(pt_sb[kb], ps[:, kb, :])
                last.then_inc(pt_evac, 1)
                if ITEMS[i // 2] == "A":
                    dve.wait_ge(sink_e, 2 * l + s + 1)
                    link(dve.tensor_add(sm[:, s, 8:12], sm[:, s, 8:12], sm[:, s, 16:20]))
                link(dve.reciprocal(sm[:, s, 20:24], sm[:, s, 8:12]))

            def soft_out(l, i):
                it, s = ITEMS[i // 2], i % 2
                n = 10 * l + i + 1
                dve.wait_ge(o_mm, n)
                o = ps[:, 2 + 2 * s, 0:256].rearrange("p (h d) -> p h d", h=4)
                r = b2(sm[:, s, 20:24], HD)
                if it not in ("B0", "B1"):
                    dve.tensor_tensor(xn[:, s, O_COL[it]:O_COL[it] + 256].rearrange("p (h d) -> p h d", h=4), o, r,
                                      ALU.mult).then_inc(o_evac, 1)
                    return
                t = otmp[:, :].rearrange("p (h m d) -> p h m d", h=2, m=2)
                dve.tensor_tensor(otmp[:, :].rearrange("p (h d) -> p h d", h=4), o, r, ALU.mult).then_inc(o_evac, 1)
                dve.wait_ge(o_evac, n)
                ob = xn[:, s, O_COL[it]:O_COL[it] + P].rearrange("p (h d) -> p h d", h=2)
                link(dve.scalar_tensor_tensor(out=ob, in0=t[:, :, 1, :], scalar=lam[:, 4:5], in1=t[:, :, 0, :],
                                              op0=ALU.mult, op1=ALU.add))
                if it == "B1":
                    o4 = xn[:, s, 256:512]
                    link(dve.tensor_mul(otmp[:, :], o4, o4))
                    st = 72 + 12 * (2 * l + s)
                    dve.tensor_reduce(stat[:, st:st + 4], otmp[:, :].rearrange("p (h d) -> p h d", h=4), AX,
                                      ALU.add).then_inc(dsq, 1)

            def residual(l, which):
                for s in range(2):
                    q = 4 * l + 2 * which + s
                    dve.wait_ge(prs, q + 1)
                    dve.wait_ge(gbs, q + 1)
                    y = ps[:, 2 + 2 * s:4 + 2 * s, :] if q < 6 else acc[s].rearrange("p (a b) -> p a b", a=2)
                    g = xn[:, s, :].rearrange("p (a b) -> p a b", a=2)
                    link(dve.scalar_tensor_tensor(out=g, in0=y, scalar=stat[:, 26 + 3 * q:27 + 3 * q], in1=g,
                                                  op0=ALU.mult, op1=ALU.mult))
                    dve.tensor_add(x[:, s, :], x[:, s, :], xn[:, s, :]).then_inc(x_upd, 1)

            def ffn():
                split_to(FFN_U + 2)

                def hidden(f):
                    dve.wait_ge(f_sil, f + 1)
                    dve.tensor_mul(hid.rearrange("p (s n) -> p s n", s=2), ps[:, 6:8, 256:512],
                                   sil.rearrange("p (s n) -> p s n", s=2)).then_inc(f_h, 1)

                def h_rest(f):
                    dve.wait_ge(f_hi, f + 1)
                    dve.tensor_sub(h_lo[:, :].rearrange("p (s n) -> p s n", s=2), ps[:, 0:2, 0:256],
                                   h_hi[:, :].rearrange("p (s n) -> p s n", s=2)).then_inc(f_lo, 1)

                hidden(0)
                with dve.Fori(0, (NFF - 1) // 2) as i:
                    for k in range(2):
                        c = FFN_U + 2 + 3 * k
                        lo(i, c)
                        lo(i, c + 1)
                        h_rest(2 * i + k)
                        lo(i, c + 2)
                        hidden(2 * i + (k + 1))
                split[0] = FFN_U + 2 + 3 * (NFF - 1)
                split_to(FFN_U + 3 * NFF)
                h_rest(NFF - 1)

            def route():
                R = [rt[:, i, :].rearrange("p (s e) -> p s e", s=2) for i in range(8)]
                col = [rt[:, 11, 2 * i:2 * i + 2] for i in range(8)]
                logit, eq, sel1, sel2, rest, mask, wt, tmp = R
                m1, t, m2, dm, ex, g1, g2, mx = col
                rev = cst[:, C_REV8:C_REV8 + 8].unsqueeze(1).to_broadcast([P, 2, NE])

                def first_max(sel, v, m):
                    link(dve.tensor_reduce(m, v, AX, ALU.max))
                    link(dve.tensor_tensor(eq, v, b2(m, NE), ALU.is_equal))
                    link(dve.tensor_tensor(eq, eq, rev, ALU.mult))
                    link(dve.tensor_reduce(t, eq, AX, ALU.max))
                    link(dve.tensor_tensor(sel, eq, b2(t, NE), ALU.is_equal))

                dve.wait_ge(r_rowT, 2)
                dve.tensor_copy(hrow[1].rearrange("p (a b) -> p a b", a=2), ps[:, 2:4, :]).then_inc(r_row, 1)
                dve.wait_ge(r_mm, 1)
                link(dve.tensor_copy(logit, ps[:, 4, 0:16].rearrange("p (s e) -> p s e", s=2)))
                first_max(sel1, logit, m1)
                link(dve.scalar_tensor_tensor(out=rest, in0=sel1, scalar=-3.0e38, in1=logit, op0=ALU.mult, op1=ALU.add))
                first_max(sel2, rest, m2)
                link(dve.tensor_add(mask, sel1, sel2))
                dve.tensor_sub(dm, m2, m1).then_inc(r_diff, 1)
                dve.wait_ge(r_exp, 1)
                link(dve.tensor_scalar(tmp[:, 0, 0:2], ex, 1.0, None, ALU.add))
                link(dve.reciprocal(g1, tmp[:, 0, 0:2]))
                link(dve.tensor_mul(g2, ex, g1))
                link(dve.tensor_tensor(wt, sel1, b2(g1, NE), ALU.mult))
                link(dve.tensor_tensor(tmp, sel2, b2(g2, NE), ALU.mult))
                link(dve.memset(comb[:, :, :], 0.0))
                link(dve.memset(pos[:, :, :, :], -1.0 - 2 * P))
                link(dve.tensor_add(comb[:, :, 0:NE], wt, tmp))
                dve.wait_ge(r_pos, 1)
                for s in range(2):
                    link(dve.scalar_tensor_tensor(out=tmp[:, s, :], in0=ps[:, 6, 8 * s:8 * s + 8], scalar=1.0,
                                                  in1=mask[:, s, :], op0=ALU.add, op1=ALU.mult))
                for p in range(2):
                    link(dve.tensor_scalar(pos[:, p, :, 0:NE], tmp, 1.0 + CAP * p, None, ALU.subtract))
                link(dve.tensor_reduce(mx[:, 0:1], ps[:, 6, 16:24], AX, ALU.max))
                dve.tensor_copy(flag[:, :], mx[:, 0:1]).then_inc(r_ready, 1)
                for s in range(2):
                    last = dve.memset(acc[s], 0.0)
                last.then_inc(m_h, 1)

            def picks(p, e):
                iota = cst[:, C_IOTA:C_IOTA + P]
                for s in range(2):
                    dve.tensor_scalar(pick[:, s, :], iota, pos[:, p, s, bass.ds(e, 1)], None, ALU.is_equal)
                    last = dve.tensor_scalar(pickw[:, s, :], iota, pos[:, p, s, bass.ds(e, 1)], comb[:, s, bass.ds(e, 1)],
                                             ALU.is_equal, ALU.mult)
                last.then_inc(m_pick, 1)

            def gathered_lo(n):
                dve.wait_ge(m_xhi, n + 1)
                dve.tensor_sub(x_lo[:, 0, :].rearrange("p (a b) -> p a b", a=2), ps[:, 4:6, :],
                               x_hi[:, 0, :].rearrange("p (a b) -> p a b", a=2)).then_inc(m_xlo, 1)

            def moe(p):
                b = MOE_U + 42 * NE * p

                def hidden(n):
                    dve.wait_ge(m_sil, n + 2)
                    dve.tensor_mul(hid, ps[:, 7, :], sil).then_inc(m_h, 1)

                def h_rest(n):
                    dve.wait_ge(m_hi, n + 1)
                    dve.tensor_sub(h_lo[:, :], ps[:, 0, :], h_hi[:, :]).then_inc(m_lo, 1)

                def y_half(e):
                    dve.wait_ge(used, 42 * e + (b + 42))
                    dve.tensor_copy(y_sb[:, 512:1024], ps[:, 3, :]).then_inc(m_y1, 1)

                def accumulate(e):
                    for s in range(2):
                        dve.wait_ge(m_c, 2 * e + (16 * p + s + 1))
                        a = acc[s].rearrange("p (a b) -> p a b", a=2)
                        dve.tensor_add(a, a, ps[:, 4 - 2 * s:6 - 2 * s, :]).then_inc(m_acc, 1)

                def expert(e, first):
                    n0 = 7 * e + 56 * p
                    lo(7 * e, b)
                    lo(7 * e, b + 1)
                    if not first:
                        y_half(e - 1)
                    for k in range(2, 5):
                        lo(7 * e, b + k)
                    if not first:
                        accumulate(e - 1)
                    lo(7 * e, b + 5)
                    hidden(n0)
                    lo(7 * e, b + 6)
                    lo(7 * e, b + 7)
                    h_rest(n0)
                    dve.wait_ge(m_bT, e + (8 * p + 1))
                    dve.wait_ge(m_gath, e + (9 * p + 1))
                    picks(p, e + 1)
                    lo(7 * e + 1, b + 2)
                    lo(7 * e + 1, b + 3)
                    hidden(n0 + 1)
                    with dve.Fori(2, NJ) as j:
                        for k in range(3):
                            lo(7 * e + j, b - 2 + k)
                        h_rest(n0 + j - 1)
                        for k in range(3, 6):
                            lo(7 * e + j, b - 2 + k)
                        hidden(n0 + j)
                    lo(7 * e, b + 40)
                    lo(7 * e, b + 41)
                    h_rest(n0 + (NJ - 1))
                    gathered_lo(e + (9 * p + 1))

                picks(p, 0)
                gathered_lo(9 * p)
                expert(0, True)
                with dve.Fori(1, NE) as e:
                    expert(e, False)
                y_half(NE - 1)
                accumulate(NE - 1)

            for l in range(DEPTH):
                lam_init = 0.8 - 0.6 * math.exp(-0.3 * l)
                for c in range(4):
                    ada(l, c)
                norm_cols(l, 0)
                for j in range(NWIN):
                    split_to(win_u(l, j) + 3)
                    dve.wait_ge(used, win_end(l, j))
                    for dst, src in proj_copies(1, j):
                        last = dve.tensor_copy(dst, src)
                    last.then_inc(win_evac[1], 1)
                dve.wait_ge(win_evac[1], NWIN * (l + 1))
                dve.wait_ge(in_layer[l], N_LAYER)
                if l == 0:
                    dve.wait_ge(in_cst, 16)
                link(rope(proj[1][:, QA:QA + 384], 6, 64))
                link(rope(proj[1][:, QB:QB + 512], 16, 32))
                link(rope(proj[1][:, KPE:KPE + 32], 1, 32))
                dve.tensor_copy(kp4[1].rearrange("p (h d) -> p h d", h=4),
                                proj[1][:, KPE:KPE + 32].unsqueeze(1).to_broadcast([P, 4, 32])).then_inc(roped, 1)
                dve.tensor_copy(kp4[2].rearrange("p (h d) -> p h d", h=4),
                                kcache[:, K_KPE:K_KPE + 32].unsqueeze(1).to_broadcast([P, 4, 32])).then_inc(kp4_ready[1], 1)
                for s in range(2):
                    dve.wait_ge(crs, 2 * l + s + 1)
                    r = 48 + 6 * (2 * l + s)
                    for o, n, g, c in ((CQ, QR, R_QN, 4), (CKV, P, R_KVN, 5)):
                        v = proj[s][:, o:o + n]
                        last = dve.scalar_tensor_tensor(out=v, in0=v, scalar=stat[:, r + c:r + c + 1], in1=par[:, g:g + n],
                                                        op0=ALU.mult, op1=ALU.mult)
                    last.then_inc(cnorm, 1)
                dve.wait_ge(cnorm, 2 * l + 2)
                for i in range(2):
                    o = R_LAM + 64 * i
                    last = dve.tensor_tensor_reduce(out=xn[:, 1, 512 + 32 * i:544 + 32 * i], in0=par[:, o:o + 32], in1=par[:, o + 32:o + 64],
                                                    scale=1.0, scalar=0.0, op0=ALU.mult, op1=ALU.add, accum_out=lam[:, i:i + 1])
                last.then_inc(lam_s, 1)
                dve.wait_ge(lam_e, l + 1)
                link(dve.scalar_tensor_tensor(out=lam[:, 4:5], in0=lam[:, 3:4], scalar=-lam_init, in1=lam[:, 2:3],
                                              op0=ALU.add, op1=ALU.subtract))
                link(dve.tensor_scalar(par[:, R_SUB:R_SUB + 64], par[:, R_SUB:R_SUB + 64], 1.0 - lam_init, None, ALU.mult))
                for k in range(np_(1)):
                    prep(l, k)
                    if k == 4:
                        ada(l, 4)
                ada(l, 5)
                soft_pre(l, 0)
                for i in range(10):
                    if i + 1 < 10:
                        soft_pre(l, i + 1)
                    soft_T(l, i)
                    if i < 6:
                        ada(l, 6 + i)
                    soft_out(l, i)
                for s in range(2):
                    n = 2 * l + s
                    dve.wait_ge(drs, n + 1)
                    o4 = xn[:, s, 256:512].rearrange("p (h d) -> p h d", h=4)
                    st = 80 + 12 * n
                    link(dve.tensor_tensor(o4, o4, b2(stat[:, st:st + 4], HD), ALU.mult))
                    dve.tensor_tensor(o4, o4, par[:, R_SUB:R_SUB + 64].unsqueeze(1).to_broadcast([P, 4, HD]),
                                      ALU.mult).then_inc(o_ready, 1)
                for s in range(2):
                    dve.wait_ge(o_hi, 2 * l + s + 1)
                    dve.tensor_sub(x_lo[:, s, :].rearrange("p (a b) -> p a b", a=2), ps[:, 6 * s:6 * s + 2, :],
                                   x_hi[:, s, :].rearrange("p (a b) -> p a b", a=2)).then_inc(o_lo, 1)
                split_to(wo_u(l, 2))
                residual(l, 0)
                norm_cols(l, 1)
                if l == 0:
                    ffn()
                    residual(0, 1)

            route()
            moe(0)
            dve.wait_ge(r_ready, 1)
            n = dve.value_load(flag[0:1, 0:1], min_val=0, max_val=2 * P)
            with dve.If(n > CAP):
                moe(1)
            dve.memset(rt[:, 10, :], 0.0).then_inc(m_done, 1)
            residual(1, 1)

        @block.tensor
        def _(pe):
            def products(t, c, tiles):
                pe.wait_ge(hi_done, 6 * t + (c + 1))
                for out, xh, xl, w, start, stop in tiles:
                    pe.matmul(out, xh, split_hi(c, w), start=start, stop=False, skip_group_check=True)
                    last = pe.matmul(out, xl, split_hi(c, w), start=False, stop=False, skip_group_check=True)
                last.then_inc(hi_used, 1)
                pe.wait_ge(lo_done, 6 * t + (c + 1))
                for out, xh, xl, w, start, stop in tiles:
                    last = pe.matmul(out, xh, split_lo(c, w), start=False, stop=stop, skip_group_check=True)
                last.then_inc(used, 1)

            def xcols(s, k):
                return x_hi[:, s, P * k:P * k + P], x_lo[:, s, P * k:P * k + P]

            pe.wait_ge(in_cst, 16)
            pe.wait_ge(cond_silu, 1)
            pe.transpose(ps[:, 7, 0:16], rows_s, ident(16))
            pe.wait_ge(in_g, 32)
            pe.transpose(ps[:, 7, 16:48], rows_g, ident(32)).then_inc(init_T, 1)

            def ada(l, c):
                a, k = 12 * l + c, c // 2
                if a == 0:
                    pe.wait_ge(init_cols, 1)
                else:
                    pe.wait_ge(row_evac, a)
                if l and c == 0:
                    pe.wait_ge(x_upd, 4)
                for h in range(2):
                    u, s = ada_u(l, c) + h, (ada_u(l, c) + h) % NSPL
                    for part, ready in ((w_hi, hi_done), (w_lo, lo_done)):
                        pe.wait_ge(ready, u + 1)
                        for kt in range(4):
                            last = pe.matmul(ps[0:CM, 7, :], cond[:, 4 * h + kt, :], part[:, s, 512 * kt:512 * kt + 512],
                                             start=h == 0 and kt == 0 and part is w_hi, stop=h == 1 and kt == 3 and part is w_lo)
                        last.then_inc(hi_used if part is w_hi else used, 1)
                if c % 2 and k not in (2, 5):
                    n = col_idx(l, k)
                    pe.wait_ge(row_evac, a + 1)
                    pe.wait_ge(in_brow[0], 16 * (n + 1))
                    if n:
                        pe.wait_ge(col_evac, n)
                    for kt in range(KT):
                        last = pe.matmul(ps[:, 6, 2 * kt:2 * kt + 2], mrow[0:5, P * kt:P * kt + P], cst[0:5, C_SEL:C_SEL + 2],
                                         start=True, stop=True)
                    last.then_inc(col_mm, 1)

            def cols(k, n):
                return slice(n * k, n * k + n)

            def norm_T(l, which):
                for s in range(2):
                    pe.wait_ge(nxn, 4 * l + 2 * which + s + 1)
                    for k in range(KT):
                        last = pe.transpose(ps[:, 2 * s + k // 4, cols(k % 4, P)], xn[:, s, cols(k, P)], ident())
                    last.then_inc(nT, 1)

            def gates(l, which):
                r = 32 + 32 * which
                pe.wait_ge(gate_ready, 2 * l + which + 1)
                for s in range(2):
                    q = 4 * l + 2 * which + s
                    if s:
                        pe.wait_ge(gbs, q)
                    for h in range(2):
                        last = pe.matmul(ps[:, 6 + h, :], cst[r:r + 5, C_SELB + P * s:C_SELB + P * s + P],
                                         mrow[r:r + 5, cols(h, 512)], start=True, stop=True)
                    last.then_inc(gb, 1)

            def prep(l, k):
                for s in range(2):
                    if k >= np_(s):
                        continue
                    step, b, nk = PREP[s][k], 2 * (k % 3) + s, nk_of(s)
                    pj = proj[s]
                    if k >= 3:
                        pe.wait_ge(prep_evac[s], np_(s) * l + k - 2)
                    elif k == 0:
                        pe.wait_ge(win_evac[s], NWIN * (l + 1))
                        if s:
                            pe.wait_ge(roped, l + 1)
                            pe.wait_ge(in_layer[l], N_LAYER)
                    o = ps[:, b, :]

                    def T(c, src, n=P):
                        return pe.transpose(o[0:n, cols(c, P)], src, ident())

                    if step == "A":
                        T(0, pj[:, QA:QA + P])
                        T(1, pj[:, QA + P:QA + 2 * P])
                        last = T(2, pj[:, KA:KA + P])
                        if s:
                            last = T(3, kcache[:, K_WK:K_WK + P])
                    elif step in ("B0", "B1"):
                        h = P * int(step[1])
                        T(0, pj[:, QB + h:QB + h + P])
                        last = T(1, pj[:, KB + h:KB + h + P])
                        if s:
                            last = T(2, kcache[:, K_DK + h:K_DK + h + P])
                    elif step == "D":
                        for r in range(2):
                            T(r, pj[:, QD + P * r:QD + P * r + P])
                            last = T(2 + r, pj[:, KD + P * r:KD + P * r + P])
                    elif step == "Dc":
                        for r in range(2):
                            last = T(r, kcache[:, K_NK + P * r:K_NK + P * r + P])
                    elif step == "C1":
                        pe.wait_ge(cnorm, 2 * l + s + 1)
                        for r in range(2):
                            T(r, pj[:, CQ + 96 * r:CQ + 96 * r + 96], 96)
                        last = T(2, pj[:, CKV:CKV + P])
                        if s:
                            last = T(3, kcache[:, K_CKV:K_CKV + P])
                    elif step == "C2":
                        pe.wait_ge(prep_evac[s], np_(s) * l + k)
                        pe.wait_ge(in_layer[l], N_LAYER)
                        for r in range(3):
                            for i in range(2):
                                cq = ct[s][0:96, cols(i, P)]
                                if r < 2:
                                    last = pe.matmul(o[:, cols(r, P)], wuq[0:96, 384 * i + P * r:384 * i + P * r + P], cq, start=i == 0, stop=i == 1)
                                else:
                                    last = pe.matmul(o[:, cols(2, P)], cq, wuq[0:96, 384 * i + 256:384 * i + 384], start=i == 0, stop=i == 1)
                    elif step in ("C3", "C4"):
                        for r in range(2):
                            if step == "C3":
                                last = pe.matmul(o[:, 256 * r:256 * r + nk], wukv[:, cols(r, P)], ct[s][:, 256:256 + nk],
                                                 start=True, stop=True)
                            elif r <= s:
                                last = pe.matmul(o[:, cols(r, 256)], ct[s][:, 256 + P * r:384 + P * r], wukv[:, 256:512],
                                                 start=True, stop=True)
                    elif step == "C5":
                        pe.wait_ge(kp4_ready[s], l + 1)
                        if s:
                            pe.wait_ge(qr_ready, l + 1)
                        T(0, small[:, P * s:P * s + P])
                        last = T(1, kp4[s])
                        if s:
                            last = T(2, kp4[2])
                    else:
                        last = pe.matmul(o, cst[:, C_ANTI:C_ANTI + P], bm, start=True, stop=True)
                    last.then_inc(prep_mm[s], 1)

            def item_scores(l, i):
                it, s = ITEMS[i // 2], i % 2
                nk, v = nk_of(s), score_view(s)
                if i < 2:
                    for t in range(2):
                        pe.wait_ge(prep_evac[t], np_(t) * (l + 1))
                else:
                    pe.wait_ge(o_evac, 10 * l + i - 1)
                for h in range(4):
                    m = 2 * (h % 2) + h // 2 if it == "A" else h
                    k = nk * (KEYS[it] + (h // 2 if it in ("C", "D") else 0))
                    last = pe.matmul(v[:, h, :], qz[:, s, QZ[it], m, :], keys[s][:, k:k + nk], start=True, stop=it != "C")
                    if it == "C":
                        k = nk * KEYS["rope"]
                        last = pe.matmul(v[:, h, :], qz[:, s, QZ["rope"], h, :], keys[s][:, k:k + nk], start=False, stop=True)
                last.then_inc(scores, 1)

            def item_T(l, i):
                n = 10 * l + i
                pe.wait_ge(probs_ready, n + 1)
                if n:
                    pe.wait_ge(pt_evac, n)
                for kb in range(1 + i % 2):
                    for h in range(4):
                        last = pe.transpose(ps[:, kb, cols(h, P)], probs[:, i % 2, h, cols(kb, P)], ident())
                last.then_inc(pT, 1)

            def item_out(l, i):
                it, s = ITEMS[i // 2], i % 2
                pe.wait_ge(pt_evac, 10 * l + i + 1)
                for h in range(4):
                    if it == "A":
                        vs = (proj[s][:, VA + HD * (h // 2):VA + HD * (h // 2) + HD],
                              vcache[:, V_W + HD * (h // 2):V_W + HD * (h // 2) + HD])
                    elif it == "D":
                        vs = (proj[s][:, VD + HD * h:VD + HD * h + HD], vcache[:, V_N + HD * h:V_N + HD * h + HD])
                    elif it == "C":
                        vs = [v_mla[s][:, cols(4 * kb + h, HD)] for kb in range(1 + s)]
                    else:
                        g = 2 * int(it[1]) + h // 2
                        vs = (proj[s][:, VB + HD * g:VB + HD * g + HD], vcache[:, V_D + HD * g:V_D + HD * g + HD])
                    for kb in range(1 + s):
                        last = pe.matmul(ps[:, 2 + 2 * s, cols(h, HD)], pt_sb[kb][:, cols(h, P)], vs[kb],
                                         start=kb == 0, stop=kb == s)
                last.then_inc(o_mm, 1)

            def attention(l):
                for k in range(np_(1)):
                    prep(l, k)
                    if k == 4:
                        ada(l, 4)
                ada(l, 5)
                item_scores(l, 0)
                for i in range(10):
                    if i + 1 < 10:
                        item_scores(l, i + 1)
                    item_T(l, i)
                    if i < 6:
                        ada(l, 6 + i)
                    item_out(l, i)

            def out_projection(l):
                for s in range(2):
                    pe.wait_ge(o_ready, 2 * l + s + 1)
                    if s == 0:
                        pe.wait_ge(pt_evac, 10 * (l + 1))
                    else:
                        pe.wait_ge(col_evac, 4 * (l + 1))
                        pe.wait_ge(row_evac, 12 * (l + 1))
                    for k in range(KT):
                        last = pe.transpose(ps[:, 6 * s + k // 4, cols(k % 4, P)], xn[:, s, cols(k, P)], ident())
                    last.then_inc(oT, 1)
                pe.wait_ge(o_evac, 10 * (l + 1))
                pe.wait_ge(o_hi, 2 * l + 2)
                pe.wait_ge(o_lo, 2 * l + 2)
                for j in range(2):
                    for h in range(2):
                        tiles = [(ps[:, 2 + 2 * s + j, :], *xcols(s, 4 * h + k), cols(k, 512), h == 0 and k == 0, h == 1 and k == 3)
                                 for s in range(2) for k in range(4)]
                        products(0, wo_u(l, j) + h, tiles)

            def dense():
                def gate_up(t, c, up):
                    products(t, c, [(ps[:, 6 + s, 256 * up:256 * up + 256], *xcols(s, k), cols(k, 256), k == 0, k == KT - 1)
                                    for s in range(2) for k in range(KT)])

                def hidden_T(f):
                    pe.wait_ge(f_h, f + 1)
                    for s in range(2):
                        for r in range(2):
                            last = pe.transpose(ps[:, s, cols(r, P)], hid[:, 256 * s + P * r:256 * s + P * r + P], ident())
                    last.then_inc(f_T, 1)

                def down(t, c, f, first=False, final=False):
                    pe.wait_ge(f_hi, f + 1)
                    pe.wait_ge(f_lo, f + 1)
                    products(t, c, [(ps[:, 2 + 2 * s + n, :], h_hi[:, 256 * s + P * r:256 * s + P * r + P],
                                     h_lo[:, 256 * s + P * r:256 * s + P * r + P], slice(1024 * r + 512 * n, 1024 * r + 512 * n + 512),
                                     first and r == 0, final and r == 1)
                                    for s in range(2) for r in range(2) for n in range(2)])

                def two_blocks(i, first):
                    for k in range(2):
                        c = FFN_U + 2 + 3 * k
                        pe.wait_ge(f_h, 2 * i + (k + 1))
                        gate_up(i, c, 0)
                        hidden_T(2 * i + k)
                        gate_up(i, c + 1, 1)
                        down(i, c + 2, 2 * i + k, first=first and k == 0)

                for s in range(2):
                    pe.wait_ge(nhi, 2 + s + 1)
                    pe.wait_ge(nlo, 2 + s + 1)
                gate_up(0, FFN_U, 0)
                gate_up(0, FFN_U + 1, 1)
                two_blocks(0, True)
                with pe.Fori(1, (NFF - 1) // 2) as i:
                    two_blocks(i, False)
                hidden_T(NFF - 1)
                down(0, FFN_U + 3 * NFF - 1, NFF - 1, final=True)

            def route():
                pe.wait_ge(in_rtr, 16)
                for s in range(2):
                    pe.wait_ge(nh, 6 + s + 1)
                for s in range(2):
                    for k in range(KT):
                        last = pe.matmul(ps[:, 4, cols(s, NE)], hT[s][:, cols(k, P)], rtr[:, k, :], start=k == 0, stop=k == KT - 1)
                last.then_inc(r_mm, 1)
                for s in range(2):
                    for k in range(KT):
                        last = pe.transpose(ps[:, 2 * s + k // 4, cols(k % 4, P)], hT[s][:, cols(k, P)], ident())
                    last.then_inc(r_rowT, 1)
                pe.wait_ge(r_diff, 1)
                up, one = cst[:, C_UP:C_UP + P], cst[:, C_ONE:C_ONE + P]
                mask = [rt[:, 5, cols(s, NE)] for s in range(2)]
                for n, pair in enumerate(((up, None), (one, up), (one, one))):
                    for s, m in enumerate(pair):
                        if m is not None:
                            last = pe.matmul(ps[:, 6, cols(n, NE)], m, mask[s], start=s == 0, stop=s == 1 or pair[1] is None)
                last.then_inc(r_pos, 1)

            def moe(p):
                b = MOE_U + 42 * NE * p

                def gather(n):
                    pe.wait_ge(m_pick, n + (9 * p + 1))
                    for k in range(KT):
                        for s in range(2):
                            last = pe.matmul(ps[:, 4 + k // 4, cols(k % 4, P)], hrow[s][:, cols(k, P)], pick[:, s, :],
                                             start=s == 0, stop=s == 1)
                    last.then_inc(m_gath, 1)

                def gate_up(t, c, up):
                    for h in range(2):
                        products(t, c + h, [(ps[:, 6 + up, :], *xcols(0, 4 * h + k), cols(k, 512), h == 0 and k == 0, h == 1 and k == 3)
                                            for k in range(4)])

                def hidden_T(n):
                    pe.wait_ge(m_h, n + 2)
                    for r in range(4):
                        last = pe.transpose(ps[:, 0, cols(r, P)], hid[:, cols(r, P)], ident())
                    last.then_inc(m_T, 1)

                def down(t, c, n, first=False, final=False):
                    pe.wait_ge(m_hi, n + 1)
                    pe.wait_ge(m_lo, n + 1)
                    for h in range(2):
                        products(t, c + h, [(ps[:, 2 + q, :], h_hi[:, cols(2 * h + r, P)], h_lo[:, cols(2 * h + r, P)],
                                             slice(1024 * r + 512 * q, 1024 * r + 512 * q + 512),
                                             first and h == 0 and r == 0, final and h == 1 and r == 1)
                                            for r in range(2) for q in range(2)])

                def combine(e):
                    pe.wait_ge(m_y0, e + (8 * p + 1))
                    pe.wait_ge(m_y1, e + (8 * p + 1))
                    pe.wait_ge(m_back, e + (8 * p + 1))
                    for s in range(2):
                        for h in range(2):
                            last = pe.matmul(ps[:, 4 - 2 * s + h, :], back[:, s, :], y_sb[:, cols(h, 512)], start=True, stop=True)
                        last.then_inc(m_c, 1)

                def expert(e, first):
                    n0 = 7 * e + 56 * p
                    pe.wait_ge(m_xhi, e + (9 * p + 1))
                    pe.wait_ge(m_xlo, e + (9 * p + 1))
                    pe.wait_ge(m_sil, n0 + 1)
                    gate_up(7 * e, b, 0)
                    pe.wait_ge(m_h, n0 + 1)
                    gate_up(7 * e, b + 2, 1)
                    if not first:
                        combine(e - 1)
                    for t in range(2):
                        last = pe.transpose(ps[:, 1, cols(t, P)], pickw[:, t, :], ident())
                    last.then_inc(m_bT, 1)
                    pe.wait_ge(m_sil, n0 + 2)
                    gate_up(7 * e + 1, b - 2, 0)
                    hidden_T(n0)
                    gate_up(7 * e + 1, b, 1)
                    if not first:
                        pe.wait_ge(m_acc, 2 * e + 16 * p)
                    elif p:
                        pe.wait_ge(m_acc, 16 * p)
                    down(7 * e + 1, b + 2, n0, first=True)
                    with pe.Fori(2, NJ) as j:
                        pe.wait_ge(m_sil, n0 + j + 1)
                        gate_up(7 * e + j, b - 2, 0)
                        hidden_T(n0 + j - 1)
                        gate_up(7 * e + j, b, 1)
                        down(7 * e + j, b + 2, n0 + j - 1)
                    hidden_T(n0 + (NJ - 1))
                    gather(e + 1)
                    down(7 * e, b + 40, n0 + (NJ - 1), final=True)

                if p == 0:
                    pe.wait_ge(r_row, 2)
                else:
                    pe.wait_ge(m_acc, 16)
                gather(0)
                expert(0, True)
                with pe.Fori(1, NE) as e:
                    expert(e, False)
                combine(NE - 1)

            for l in range(DEPTH):
                if l == 0:
                    norm_T(0, 0)
                for c in range(4):
                    ada(l, c)
                if l == 1:
                    norm_T(1, 0)
                for s in range(2):
                    pe.wait_ge(nhi, 4 * l + s + 1)
                    pe.wait_ge(nlo, 4 * l + s + 1)
                for j in range(NWIN):
                    if j >= 2:
                        for s in range(2):
                            pe.wait_ge(win_evac[s], NWIN * l + j - 1)
                    for h in range(2):
                        products(0, win_u(l, j) + h,
                                 [(ps[:, 2 + 2 * (j % 2) + s, 0:WIN_N], *xcols(s, 4 * h + k), cols(k, WIN_N),
                                   h == 0 and k == 0, h == 1 and k == 3) for s in range(2) for k in range(4)])
                attention(l)
                out_projection(l)
                gates(l, 0)
                norm_T(l, 1)
                if l == 0:
                    dense()
                    gates(0, 1)

            route()
            moe(0)
            pe.wait_ge(r_ready, 1)
            n = pe.value_load(flag[0:1, 0:1], min_val=0, max_val=2 * P)
            with pe.If(n > CAP):
                moe(1)
            pe.wait_ge(m_done, 1)
            gates(1, 1)


_INS = ["x_prompt", "x_sample", "cache_win_k", "cache_win_v", "cache_diff_k", "cache_diff_v", "cache_mla_ckv",
        "cache_mla_kpe", "cache_na_k", "cache_na_v", "c", "c_ctx", "w_ada", "b_ada", "norm_mix_pre", "norm_mix_post",
        "norm_ffn_pre", "norm_ffn_post", "w_in", "w_o", "win_sink", "diff_lq1", "diff_lk1", "diff_lq2", "diff_lk2",
        "diff_subln", "mla_q_norm", "mla_kv_norm", "mla_wuq", "mla_wukv", "na_rpb", "ffn_w_gate", "ffn_w_up",
        "ffn_w_down", "moe_router", "moe_w_gate", "moe_w_up", "moe_w_down"]
_OUTS = [(1, P, D), (1, P, D), (1, DEPTH, 2, P, HD), (1, DEPTH, 2, P, HD), (1, DEPTH, 4, P, HD), (1, DEPTH, 4, P, HD),
         (1, DEPTH, P, P), (1, DEPTH, P, 32), (1, DEPTH, 4, P, HD), (1, DEPTH, 4, P, HD)]


def kernel(**inputs):
    import concourse.bacc as _bacc
    from concourse.bass_utils import run_bass_kernel_spmd as _run

    nc = _bacc.Bacc("TRN2", target_bir_lowering=False, num_devices=1)
    arrays, ins, outs = {}, [], []
    for name in _INS + ["constants"]:
        a = constants() if name == "constants" else np.ascontiguousarray(inputs[name])
        arrays[f"in_{name}"] = a
        ins.append(nc.dram_tensor(f"in_{name}", a.shape, mybir.dt.from_np(a.dtype), kind="ExternalInput").ap())
    for i, shape in enumerate(_OUTS):
        outs.append(nc.dram_tensor(f"out_{i}", shape, F32, kind="ExternalOutput").ap())
    program(nc, ins, outs)
    r = _run(nc, [arrays], core_ids=[0])
    return tuple(r.results[0][f"out_{i}"] for i in range(len(_OUTS)))
```

```python
import math
from contextlib import ExitStack

import numpy as np
import concourse.bass as bass
from concourse import mybir

F32 = mybir.dt.float32
F32R = mybir.dt.float32r
I32 = mybir.dt.int32
ALU = mybir.AluOpType
ACT = mybir.ActivationFunctionType
AX = mybir.AxisListType.X

P = 128
D = 1024
KT = D // P
DEPTH = 2
EPS = 1e-6
GRID_W = 64
HD = 64
NA_COLS = 16
RPB_R, RPB_C = 15, 31
IN_W = 2400
FF = 2816
NE = 8
FE = 3584
QR = 192
CM = 72
UNIT = 2048
NRAW = 6
NSPL = 2
WIN_N = 480
NWIN = IN_W // WIN_N
NFF = FF // 256
NJ = FE // 512
CAP = P

QA, KA, VA, QB, KB, VB, CQ, CKV, KPE, QD, KD, VD = 0, 256, 384, 512, 768, 1024, 1280, 1472, 1600, 1632, 1888, 2144

C_ID, C_UP, C_ONE, C_IOTA, C_ANTI, C_MASK = 0, 128, 256, 384, 512, 640
C_COS64, C_SIN64, C_COS32, C_SIN32, C_REV8, C_NEGH, C_SEL = 768, 832, 896, 928, 960, 968, 970
C_N = C_SEL + 2

KEYS = {"A": 0, "B0": 1, "B1": 2, "D": 3, "C": 5, "rope": 7}
QZ = {"A": 0, "D": 1, "C": 2, "B0": 3, "B1": 4, "rope": 5}
O_COL = {"A": 0, "B0": 256, "B1": 384, "C": 512, "D": 768}

K_WK, K_DK, K_NK, K_CKV, K_KPE, K_N = 0, 128, 384, 640, 768, 800
V_W, V_D, V_N, V_ALL = 0, 128, 384, 640
R_SINK, R_LAM, R_SUB, R_QN, R_KVN, R_N = 0, 4, 132, 196, 388, 516

ITEMS = ["A", "B0", "B1", "D", "C"]
PREP = [["A", "B0", "B1", "D", "C1", "C2", "C3", "C4", "C5"],
        ["A", "B0", "B1", "D", "C1", "C2", "C3", "C4", "C5", "Dc", "BM"]]
SCALE = {"A": HD ** -0.5, "B0": 32 ** -0.5, "B1": 32 ** -0.5, "D": HD ** -0.5, "C": 96 ** -0.5}


def constants():
    c = np.zeros((P, C_N), np.float32)
    i = np.arange(P)
    c[:, C_ID:C_ID + P] = np.eye(P)
    c[:, C_UP:C_UP + P] = i[:, None] < i[None, :]
    c[:, C_ONE:C_ONE + P] = 1.0
    c[:, C_IOTA:C_IOTA + P] = i[None, :]
    c[:, C_ANTI:C_ANTI + P] = (i[:, None] // GRID_W == i[None, :] // GRID_W) & \
        (i[:, None] % GRID_W + i[None, :] % GRID_W == GRID_W - 1)
    qc, kc = i[:, None] % GRID_W, i[None, :] % GRID_W
    start = np.clip(qc - NA_COLS // 2, 0, GRID_W - NA_COLS)
    c[:, C_MASK:C_MASK + P] = np.where((kc >= start) & (kc < start + NA_COLS), 0.0, -1e30)
    for width, cc, sc in ((64, C_COS64, C_SIN64), (32, C_COS32, C_SIN32)):
        h = width // 2
        inv = np.float32(10000.0) ** (-np.arange(0, h, 2, dtype=np.float32) / np.float32(h))
        for half, pos in ((0, i // GRID_W), (1, i % GRID_W)):
            ang = pos.astype(np.float32)[:, None] * inv[None, :]
            o = half * h
            c[:, cc + o:cc + o + h] = np.concatenate([np.cos(ang), np.cos(ang)], 1)
            c[:, sc + o:sc + o + h] = np.concatenate([-np.sin(ang), np.sin(ang)], 1)
    c[:, C_REV8:C_REV8 + 8] = 8 - np.arange(8)
    for s in range(2):
        c[s, C_SEL + s] = c[s + 2, C_SEL + s] = 1.0
    c[:, C_NEGH] = -0.5
    return c


BASE = [0, 38 + 3 * NFF]
FFN_U = BASE[0] + 38
MOE_U = BASE[1] + 38


def ada_u(l, c):
    return BASE[l] + 2 * c + (0 if c < 4 else 2 * NWIN if c < 10 else 2 * NWIN + 4)


def win_u(l, j):
    return BASE[l] + 8 + 2 * j


def wo_u(l, j):
    return BASE[l] + 20 + 2 * NWIN + 2 * j


def win_end(l, j):
    return win_u(l, j) + 2


def y_end(l, which):
    return FFN_U + 3 * NFF if which else wo_u(l, 1) + 2


def bcast_row(src, l, n, parts=P):
    return bass.AP(tensor=src.tensor, offset=l * n, ap=[[0, parts], [1, n]])



def program(nc, ins, outs):
    (x_prompt, x_sample, cwk, cwv, cdk, cdv, cckv, ckpe, cnk, cnv, c_lat, c_ctx, w_ada, b_ada,
     n_mix_pre, n_mix_post, n_ffn_pre, n_ffn_post, w_in, w_o, win_sink, lq1, lk1, lq2, lk2, subln,
     q_norm, kv_norm, wuq_d, wukv_d, rpb, fwg, fwu, fwd, router, mwg, mwu, mwd, consts) = ins
    (y_prompt, y_sample, nwk, nwv, ndk, ndv, nckv, nkpe, nnk, nnv) = outs

    with ExitStack() as ctx:
        def sb(name, shape, dt=F32):
            return ctx.enter_context(nc.sbuf_tensor(name, shape, dt))

        def sem(name):
            return ctx.enter_context(nc.semaphore(name))

        raw = sb("raw", [P, NRAW, UNIT])
        w_hi = sb("w_hi", [P, NSPL, UNIT], F32R)
        w_lo = sb("w_lo", [P, NSPL, UNIT], F32R)
        cst = sb("cst", [P, C_N])
        x = sb("x", [P, 2, D])
        xn = sb("xn", [P, 2, D])
        x_hi = sb("x_hi", [P, 2, D], F32R)
        x_lo = sb("x_lo", [P, 2, D], F32R)
        cond = sb("cond", [P, KT, CM], F32R)
        mrow = sb("mrow", [4, D])
        mod = sb("mod", [P, DEPTH, 6, KT, 2])
        mtmp = sb("mtmp", [P, KT, 2])
        bcol = sb("bcol", [P, DEPTH, 6, KT])
        gcol = sb("gcol", [P, 4, DEPTH, KT])
        stat = sb("stat", [P, 144])
        par = sb("par", [P, R_N])
        small = sb("small", [P, 256])
        otmp = sb("otmp", [P, 256])
        sm = sb("sm", [P, 2, 32])
        lam = sb("lam", [P, 8])
        qz = sb("qz", [P, 2, 6, 4, P])
        h_hi = sb("h_hi", [P, 512], F32R)
        h_lo = sb("h_lo", [P, 512], F32R)
        pos = sb("pos", [P, 2, 2, NE + 1])
        comb = sb("comb", [P, 2, NE + 1])
        flag = sb("flag", [P, 1], I32)
        REGION = 11904
        region = sb("region", [P, REGION])
        proj = [region[:, s * IN_W:(s + 1) * IN_W] for s in range(2)]
        o1 = 2 * IN_W
        keys = [region[:, o1 + 1024 * s:o1 + 1024 + 2048 * s] for s in range(2)]
        o2 = o1 + 3072
        v_mla = [region[:, o2 + 256 * s:o2 + 256 + 512 * s] for s in range(2)]
        bm = region[:, o2 + 768:o2 + 1280]
        vcache = region[:, o2 + 1280:o2 + 1280 + V_ALL]
        o3 = o2 + 1280 + V_ALL
        kcache = region[:, o3:o3 + K_N]
        wuq = region[:, o3 + K_N:o3 + K_N + 768]
        wukv = region[:, o3 + K_N + 768:o3 + K_N + 1280]
        probs = region[:, o3:o3 + 2048].rearrange("p (s h k) -> p s h k", s=2, h=4)
        assert o3 + K_N + 1280 <= REGION, o3 + K_N + 1280
        pt_sb = [proj[1][:, QB:QB + 512], proj[1][:, QD:QD + 512]]
        ct = [xn[:, s, 512:1024] for s in range(2)]
        hT = [region[:, D * s:D * (s + 1)] for s in range(2)]
        hrow = [region[:, 2048 + D * s:2048 + D * (s + 1)] for s in range(2)]
        sil = region[:, 4096:4608]
        hid = region[:, 4608:5120]
        y_sb = region[:, 5120:6144]
        acc = [region[:, 6144 + D * s:6144 + D * (s + 1)] for s in range(2)]
        pick = region[:, 8192:8448].rearrange("p (s c) -> p s c", s=2)
        pickw = region[:, 8448:8704].rearrange("p (s c) -> p s c", s=2)
        back = region[:, 8704:8960].rearrange("p (s c) -> p s c", s=2)
        hTn = [region[:, o1 + D * s:o1 + D * (s + 1)] for s in range(2)]
        rt = region[:, 8960:9152].rearrange("p (a b) -> p a b", a=12)
        rtr = region[:, 9152:9216].rearrange("p (k e) -> p k e", k=KT)
        kp4 = [xn[:, 0, 384:512], xn[:, 1, 0:128], xn[:, 1, 128:256]]
        rows_c = region[0:16, 9000:9128]
        rows_s = region[0:16, 9128:9256]
        rows_g = region[0:64, 9256:9384]
        rows_b = region[0:96, 9384:9512]
        def gdiag(q):
            o = 2048 if q >= 6 else 6144
            return region[:, o + D * (q % 2):o + D * (q % 2) + D]

        junk = region[:, 4096:5120]

        ps = ctx.enter_context(nc.psum_tensor("ps", [P, 8, 512], F32))

        def ident(n=P):
            return cst[0:n, C_ID:C_ID + n]

        def h_of(l, which):
            return hT if which else hTn

        raw_in = [sem(f"raw_in{i}") for i in range(NRAW)]
        hi_done, lo_done, hi_used, used = sem("hi_done"), sem("lo_done"), sem("unit_hi_used"), sem("unit_used")
        in_cst, in_c, in_g = sem("in_cst"), sem("in_c"), sem("in_g")
        in_x = [sem("in_x0"), sem("in_x1")]
        in_rtr = sem("in_rtr")
        in_layer = [sem("in_layer0"), sem("in_layer1")]
        cond_T, cond_ready = sem("cond_T"), sem("cond_ready")
        qz_zero, cond_silu, init_T, init_cols = sem("qz_zero"), sem("cond_silu"), sem("init_T"), sem("init_cols")
        row_evac, col_mm, mod_ready, diag_ready = sem("row_evac"), sem("col_mm"), sem("mod_ready"), sem("gate_diag_ready")
        nsq, nrs, nxn, nT, nh, nhi, nlo = (sem(n) for n in ("norm_sq", "norm_rstd", "norm_rows", "norm_T", "norm_h", "norm_hi", "norm_lo"))
        win_evac = [sem("win_evac0"), sem("win_evac1")]
        roped, kp4_ready = sem("roped"), [sem("kp4_ready0"), sem("kp4_ready1")]
        csq, crs = sem("c_sq"), sem("c_rstd")
        cnorm = sem("c_norm")
        m_done = sem("moe_done")
        qr_ready = sem("qr_ready")
        prep_mm = [sem("prep_mm0"), sem("prep_mm1")]
        prep_evac = [sem("prep_evac0"), sem("prep_evac1")]
        scores, sm_bias, probs_ready, pT, pt_evac, o_mm, o_evac = (sem(n) for n in ("scores", "softmax_bias", "probs_ready", "probs_T", "probs_T_evac", "o_mm", "o_evac"))
        sink_d, sink_e = sem("sink_arg"), sem("sink_exp")
        lam_s, lam_e = sem("lam_sums"), sem("lam_exp")
        dsq, drs, o_ready, oT, o_hi, o_lo = (sem(n) for n in ("diff_sq", "diff_rstd", "o_ready", "o_T", "o_hi", "o_lo"))
        psq, prs, gb, gbs, x_upd = (sem(n) for n in ("post_sq", "post_rstd", "gate_bcast", "gate_bcast_sbuf", "x_updated"))
        f_sil, f_h, f_T, f_hi, f_lo = (sem(n) for n in ("ffn_silu", "ffn_h", "ffn_hT", "ffn_h_hi", "ffn_h_lo"))
        r_mm, r_rowT, r_row, r_diff, r_exp, r_pos, r_ready = (sem(n) for n in ("rt_logits", "rt_rows", "rt_rows_evac", "rt_diff", "rt_exp", "rt_pos", "rt_ready"))
        m_pick, m_gath, m_xhi, m_xlo, m_pw, m_bT, m_back = (sem(n) for n in ("moe_pick", "moe_gather", "moe_x_hi", "moe_x_lo", "moe_pick_w", "moe_back_T", "moe_back"))
        m_sil, m_h, m_T, m_hi, m_lo = (sem(n) for n in ("moe_silu", "moe_h", "moe_hT", "moe_h_hi", "moe_h_lo"))
        m_y0, m_y1, m_c, m_acc = (sem(n) for n in ("moe_y_half0", "moe_y_half1", "moe_comb", "moe_acc"))
        out_ctx = [sem("out_ctx0"), sem("out_ctx1")]
        out_x = sem("out_x")
        pool_step, act_step, dve_step = sem("pool_step"), sem("act_step"), sem("dve_step")
        NOUT = 8 * 16
        N_LAYER = (6 + 2 + 6 + 8 + 4) * 16

        def ada_ps(k):
            return ps[:, 6, 64 + 16 * k:80 + 16 * k]

        def np_(s):
            return len(PREP[s])

        def nk_of(s):
            return P * (1 + s)

        def prep_copies(s, step, b):
            nk, k = nk_of(s), keys[s]

            def halves(i, src):
                return [(qz[64 * g:64 * g + 64, s, i, g:4:2, :],
                         ps[64 * g:64 * g + 64, b, src:src + 256].rearrange("p (r q) -> p r q", r=2)) for g in range(2)]

            def quarters(i):
                return [(qz[32 * j:32 * j + 32, s, i, j, :], ps[32 * j:32 * j + 32, b, 0:P]) for j in range(4)]

            def blocks(n, count=1):
                return k[:, KEYS[n] * nk:(KEYS[n] + count) * nk]

            def pairs(n, src, nks):
                return (blocks(n, 2).rearrange("p (r k) -> p r k", r=2)[:, :, nks:nks + src.shape[2]], src)

            if step == "A":
                return halves(QZ["A"], 0) + [(blocks("A"), ps[:, b, 256:256 + nk])]
            if step in ("B0", "B1"):
                return quarters(QZ[step]) + [(blocks(step), ps[:, b, P:P + nk])]
            if step == "D":
                return halves(QZ["D"], 0) + [pairs("D", ps[:, b, 256:512].rearrange("p (r k) -> p r k", r=2), 0)]
            if step == "Dc":
                return [pairs("D", ps[:, b, 0:256].rearrange("p (r k) -> p r k", r=2), P)]
            if step == "C1":
                return [(ct[s][0:96, 0:256], ps[0:96, b, 0:256]), (ct[s][:, 256:256 + nk], ps[:, b, 256:256 + nk])]
            if step == "C2":
                return [(small[:, P * s:P * s + P], ps[:, b, 256:384])] + halves(QZ["C"], 0)
            if step == "C3":
                return [pairs("C", ps[:, b, :].rearrange("p (r k) -> p r k", r=2)[:, :, 0:nk], 0)]
            if step == "C4":
                return [(v_mla[s][:, 0:2 * nk], ps[:, b, 0:2 * nk])]
            return quarters(QZ["rope"]) + [(blocks("rope"), ps[:, b, P:P + nk])]

        def proj_copies(s, j):
            src = ps[:, 2 + 2 * (j % 2) + s, :]
            o = WIN_N * j
            if j:
                return [(proj[s][:, o:o + WIN_N], src[:, 0:WIN_N])]
            return [(proj[s][:, 0:256].rearrange("p (r g d) -> p r g d", r=2, g=2),
                     src[:, 0:256].rearrange("p (g r d) -> p r g d", r=2, g=2)),
                    (proj[s][:, 256:WIN_N], src[:, 256:WIN_N])]

        def score_view(s):
            if s == 0:
                return ps[:, 2, :].rearrange("p (h k) -> p h k", h=4)
            return ps[:, 4:6, :].rearrange("p a (b k) -> p (a b) k", b=2)

        def width(u):
            return 4 * WIN_N if any(win_u(l, 0) <= u < win_u(l, NWIN) for l in range(DEPTH)) else UNIT

        def split_hi(c, n):
            return w_hi[:, c % NSPL, n]

        def split_lo(c, n):
            return w_lo[:, c % NSPL, n]

        block = ctx.enter_context(nc.Block())

        @block.sync
        def _(sp):
            def load(u, slot, dst, src):
                if not (isinstance(u, int) and u < NRAW):
                    sp.wait_ge(lo_done, u - NRAW + 1)
                sp.dma_start(dst, src).then_inc(raw_in[slot], 16)

            def load_k(u, src, rows0, cols, col0=0):
                dst = raw[:, u % NRAW, 0:4 * cols].rearrange("p (k n) -> p k n", k=4)
                load(u, u % NRAW, dst, src[rows0:rows0 + 512, col0:col0 + cols].rearrange("(k p) n -> p k n", p=P))

            def ada(l, c):
                for h in range(2):
                    load_k(ada_u(l, c) + h, w_ada[l], 512 * h, 512, 512 * c)

            for l in range(DEPTH):
                for c in range(4):
                    ada(l, c)
                for j in range(NWIN):
                    for h in range(2):
                        load_k(win_u(l, j) + h, w_in[l], 512 * h, WIN_N, WIN_N * j)
                for c in range(4, 10):
                    ada(l, c)
                for j in range(2):
                    for h in range(2):
                        load_k(wo_u(l, j) + h, w_o[l], 512 * h, 512, 512 * j)
                for c in range(10, 12):
                    ada(l, c)
                if l == 0:
                    def ffn_gu(u, slot, w, f):
                        load(u, slot, raw[:, slot, :].rearrange("p (k n) -> p k n", k=KT),
                             w[0, :, bass.ds(256 * f, 256)].rearrange("(k p) n -> p k n", p=P))

                    def ffn_d(u, slot, f):
                        load(u, slot, raw[:, slot, :].rearrange("p (t n) -> p t n", t=2),
                             fwd[0, bass.ds(256 * f, 256), :].rearrange("(t p) n -> p t n", p=P))

                    ffn_gu(FFN_U, FFN_U % NRAW, fwg, 0)
                    ffn_gu(FFN_U + 1, (FFN_U + 1) % NRAW, fwu, 0)
                    with sp.Fori(0, (NFF - 1) // 2) as i:
                        for k in range(2):
                            u, s0 = 6 * i + (FFN_U + 2 + 3 * k), FFN_U + 2 + 3 * k
                            ffn_gu(u, s0 % NRAW, fwg, 2 * i + (k + 1))
                            ffn_gu(u + 1, (s0 + 1) % NRAW, fwu, 2 * i + (k + 1))
                            ffn_d(u + 2, (s0 + 2) % NRAW, 2 * i + k)
                    ffn_d(FFN_U + 3 * NFF - 1, (FFN_U + 3 * NFF - 1) % NRAW, NFF - 1)

            def moe_gu(u, slot, w, e, j, h):
                load(u, slot, raw[:, slot, :].rearrange("p (k n) -> p k n", k=4),
                     w[0, bass.ds(e, 1), 512 * h:512 * h + 512, bass.ds(512 * j, 512)]
                     .rearrange("a (k p) n -> p (a k) n", p=P))

            def moe_d(u, slot, e, j, h):
                load(u, slot, raw[:, slot, :].rearrange("p (t n) -> p t n", t=2),
                     mwd[0, bass.ds(e, 1), bass.ds(512 * j + 256 * h, 256), :]
                     .rearrange("a (t p) n -> p (a t) n", p=P))

            def moe_pass(p):
                b = MOE_U + p * 42 * NE
                with sp.Fori(0, NE) as e:
                    for k, w in ((0, mwg), (2, mwu)):
                        for h in range(2):
                            moe_gu(42 * e + (b + k + h), (b + k + h) % NRAW, w, e, 0, h)
                    with sp.Fori(1, NJ) as j:
                        for k, w in ((0, mwg), (2, mwu)):
                            for h in range(2):
                                moe_gu(42 * e + 6 * j + (b - 2 + k + h), (b + 4 + k + h) % NRAW, w, e, j, h)
                        for h in range(2):
                            moe_d(42 * e + 6 * j + (b + 2 + h), (b + 8 + h) % NRAW, e, j - 1, h)
                    for h in range(2):
                        moe_d(42 * e + (b + 40 + h), (b + 40 + h) % NRAW, e, NJ - 1, h)

            moe_pass(0)
            sp.wait_ge(r_ready, 1)
            n = sp.value_load(flag[0:1, 0:1], min_val=0, max_val=2 * P)
            with sp.If(n > CAP):
                moe_pass(1)
            for s, y in ((0, y_prompt), (1, y_sample)):
                sp.wait_ge(x_upd, 7 + s)
                sp.dma_start(y[0], x[:, s, :]).then_inc(out_x, 16)
            sp.wait_ge(out_x, 32)
            for l in range(DEPTH):
                sp.wait_ge(out_ctx[l], NOUT)

        @block.gpsimd
        def _(pool):
            steps = [0]

            def link(i):
                steps[0] += 1
                i.then_inc(pool_step, 1)
                pool.wait_ge(pool_step, steps[0])

            pool.dma_start(rows_c[0:8, :], c_ctx.rearrange("(k n) -> k n", k=KT)).then_inc(in_c, 16)
            pool.dma_start(rows_c[8:16, :], c_lat[0].rearrange("(k n) -> k n", k=KT)).then_inc(in_c, 16)
            pool.dma_start(cst[:, :], consts).then_inc(in_cst, 16)
            pool.dma_start(x[:, 0, :], x_prompt[0]).then_inc(in_x[0], 16)
            pool.dma_start(x[:, 1, :], x_sample[0]).then_inc(in_x[1], 16)
            for i, v in enumerate((n_mix_pre, n_mix_post, n_ffn_pre, n_ffn_post)):
                pool.dma_start(rows_g[16 * i:16 * i + 16, :], v.rearrange("l (k n) -> (l k) n", k=KT)).then_inc(in_g, 16)
            pool.dma_start(rows_b, b_ada.rearrange("l (k n) -> (l k) n", n=P)).then_inc(in_g, 16)

            def rstd(dst, tmp, ssq, width, done):
                link(pool.tensor_scalar(tmp, ssq, 1.0 / width, EPS, ALU.mult, ALU.add))
                n = tmp.shape[-1]
                i = pool.tensor_tensor(dst, tmp, cst[:, C_NEGH:C_NEGH + 1].to_broadcast([P, n]), ALU.pow)
                if done is not None:
                    i.then_inc(done, 1)
                return i

            def norm(l, which):
                for s in range(2):
                    q = 4 * l + 2 * which + s
                    pool.wait_ge(nsq, q + 1)
                    rstd(stat[:, 3 * q + 2:3 * q + 3], stat[:, 3 * q + 1:3 * q + 2], stat[:, 3 * q:3 * q + 1], D, nrs)

            def post(l, which):
                for s in range(2):
                    q = 4 * l + 2 * which + s
                    pool.wait_ge(psq, q + 1)
                    o = 24 + 3 * q
                    rstd(stat[:, o + 2:o + 3], stat[:, o + 1:o + 2], stat[:, o:o + 1], D, prs)

            def layer_loads(l):
                q = in_layer[l]
                if l:
                    pool.wait_ge(o_ready, 2)
                    pool.wait_ge(pt_evac, 10)
                else:
                    pool.wait_ge(init_cols, 1)
                for dst, src in ((kcache[:, K_WK:K_WK + 128], cwk), (kcache[:, K_DK:K_DK + 256], cdk),
                                 (kcache[:, K_NK:K_NK + 256], cnk), (vcache[:, V_W:V_W + 128], cwv),
                                 (vcache[:, V_D:V_D + 256], cdv), (vcache[:, V_N:V_N + 256], cnv)):
                    pool.dma_start(dst.rearrange("p (h d) -> p h d", d=HD),
                                   src[0, l].rearrange("h t d -> t h d")).then_inc(q, 16)
                pool.dma_start(kcache[:, K_CKV:K_CKV + 128], cckv[0, l]).then_inc(q, 16)
                pool.dma_start(kcache[:, K_KPE:K_KPE + 32], ckpe[0, l]).then_inc(q, 16)
                for i in range(2):
                    src = wuq_d[l, 96 * i:96 * i + 96, :].rearrange("p (h d) -> p h d", h=4)
                    o = 384 * i
                    pool.dma_start(wuq[0:96, o:o + 256].rearrange("p (h d) -> p h d", h=4), src[:, :, 0:HD]).then_inc(q, 16)
                    pool.dma_start(wuq[0:96, o + 256:o + 384].rearrange("p (h d) -> p h d", h=4), src[:, :, HD:96]).then_inc(q, 16)
                src = wukv_d[l].rearrange("p (h d) -> p h d", h=4)
                pool.dma_start(wukv[:, 0:256].rearrange("p (h d) -> p h d", h=4), src[:, :, 0:HD]).then_inc(q, 16)
                pool.dma_start(wukv[:, 256:512].rearrange("p (h d) -> p h d", h=4), src[:, :, HD:P]).then_inc(q, 16)
                for o, n, v in ((R_SINK, 4, win_sink), (R_LAM, 32, lq1), (R_LAM + 32, 32, lk1), (R_LAM + 64, 32, lq2),
                                (R_LAM + 96, 32, lk2), (R_SUB, 64, subln), (R_QN, QR, q_norm), (R_KVN, P, kv_norm)):
                    pool.dma_start(par[:, o:o + n], bcast_row(v, l, n)).then_inc(q, 16)
                for qr in range(2):
                    for kr in range(2):
                        first = (l * 4 * RPB_R + kr - qr + 7) * RPB_C - (GRID_W - 1) + NA_COLS - 1
                        pool.dma_start(bm[64 * qr:64 * qr + 64, :].rearrange("p (h k) -> p h k", h=4)[:, :, 64 * kr:64 * kr + 64],
                                       bass.AP(tensor=rpb.tensor, offset=first,
                                               ap=[[1, 64], [RPB_R * RPB_C, 4], [1, 64]])).then_inc(q, 16)

            def context_outputs(l):
                pool.wait_ge(win_evac[0], NWIN * (l + 1))
                for o, n, dst in ((KA, 2, nwk), (VA, 2, nwv), (KB, 4, ndk), (VB, 4, ndv), (KD, 4, nnk), (VD, 4, nnv)):
                    pool.dma_start(dst[0, l].rearrange("h t d -> t h d"),
                                   proj[0][:, o:o + n * HD].rearrange("p (h d) -> p h d", d=HD)).then_inc(out_ctx[l], 16)
                pool.dma_start(nkpe[0, l], proj[0][:, KPE:KPE + 32]).then_inc(out_ctx[l], 16)
                pool.wait_ge(cnorm, 2 * l + 1)
                pool.dma_start(nckv[0, l], proj[0][:, CKV:CKV + P]).then_inc(out_ctx[l], 16)

            for l in range(DEPTH):
                if l == 0:
                    pool.memset(qz[:, :, :, :, :], 0.0).then_inc(qz_zero, 1)
                    norm(0, 0)
                    layer_loads(0)
                if l:
                    norm(l, 0)
                for s in range(2):
                    n = 2 * l + s
                    pool.wait_ge(csq, n + 1)
                    o = 48 + 6 * n
                    link(pool.tensor_scalar(stat[:, o + 2:o + 3], stat[:, o:o + 1], 1.0 / QR, EPS, ALU.mult, ALU.add))
                    link(pool.tensor_scalar(stat[:, o + 3:o + 4], stat[:, o + 1:o + 2], 1.0 / P, EPS, ALU.mult, ALU.add))
                    pool.tensor_tensor(stat[:, o + 4:o + 6], stat[:, o + 2:o + 4],
                                       cst[:, C_NEGH:C_NEGH + 1].to_broadcast([P, 2]), ALU.pow).then_inc(crs, 1)
                context_outputs(l)
                for s in range(2):
                    n = 2 * l + s
                    pool.wait_ge(dsq, n + 1)
                    o = 72 + 12 * n
                    rstd(stat[:, o + 8:o + 12], stat[:, o + 4:o + 8], stat[:, o:o + 4], HD, drs)
                post(l, 0)
                norm(l, 1)
                if l == 0:
                    layer_loads(1)
                    post(0, 1)
            pool.wait_ge(x_upd, 6)
            pool.dma_start(rtr, router[0].rearrange("(k p) e -> p k e", p=P)).then_inc(in_rtr, 16)
            post(1, 1)


        @block.scalar
        def _(act):
            split = [0]

            def hi(t, c):
                act.wait_ge(raw_in[c % NRAW], 16 * t + 16 * (c // NRAW + 1))
                n = c - NSPL + 1
                if n > 0:
                    act.wait_ge(hi_used, 6 * t + n)
                    act.wait_ge(lo_done, 6 * t + n)
                act.activation(split_hi(c, slice(0, width(c))), raw[:, c % NRAW, 0:width(c)], ACT.Copy).then_inc(hi_done, 1)

            def split_to(end):
                for u in range(split[0], end):
                    hi(0, u)
                split[0] = max(split[0], end)

            steps = [0]

            def link(i):
                steps[0] += 1
                i.then_inc(act_step, 1)
                act.wait_ge(act_step, steps[0])

            act.wait_ge(in_c, 32)
            act.activation(rows_s, rows_c, ACT.Silu).then_inc(cond_silu, 1)

            def rows(l, c):
                n = 6 * l + c // 2
                if c % 2 == 0 and n:
                    act.wait_ge(col_mm, n)
                act.wait_ge(used, ada_u(l, c) + 2)
                act.activation(mrow[:, 512 * (c % 2):512 * (c % 2) + 512], ps[0:4, 7, :], ACT.Copy).then_inc(row_evac, 1)

            def norm_rows(l, which):
                for s in range(2):
                    q = 4 * l + 2 * which + s
                    if q < 2:
                        act.wait_ge(in_x[s], 16)
                    else:
                        act.wait_ge(x_upd, q - 1)
                    act.activation(xn[:, s, :], x[:, s, :], ACT.Square, accum_out=stat[:, 3 * q:3 * q + 1]).then_inc(nsq, 1)
                for s in range(2):
                    q = 4 * l + 2 * which + s
                    act.wait_ge(nrs, q + 1)
                    act.activation(xn[:, s, :], x[:, s, :], ACT.Copy, scale=stat[:, 3 * q + 2:3 * q + 3]).then_inc(nxn, 1)

            def norm_hi(l, which):
                for s in range(2):
                    act.wait_ge(nh, 4 * l + 2 * which + s + 1)
                    act.activation(x_hi[:, s, :], h_of(l, which)[s], ACT.Copy).then_inc(nhi, 1)

            def prep(l, k):
                act.wait_ge(prep_mm[0], np_(0) * l + k + 1)
                if l == 0 and k == 0:
                    act.wait_ge(qz_zero, 1)
                for dst, src in prep_copies(0, PREP[0][k], 2 * (k % 3)):
                    last = act.activation(dst, src, ACT.Copy)
                last.then_inc(prep_evac[0], 1)

            def exps(l, i):
                it, s = ITEMS[i // 2], i % 2
                act.wait_ge(sm_bias, 10 * l + i + 1)
                nk = nk_of(s)
                biased = it == "D" and s == 1
                for h in range(4):
                    src = probs[:, s, h, 0:nk] if biased else score_view(s)[:, h, :]
                    last = act.activation(probs[:, s, h, 0:nk], src, ACT.Exp, bias=sm[:, s, 4 + h:5 + h],
                                          scale=1.0 if biased else SCALE[it], accum_out=sm[:, s, 8 + h:9 + h])
                last.then_inc(probs_ready, 1)
                if it == "A":
                    act.wait_ge(sink_d, 2 * l + s + 1)
                    act.activation(sm[:, s, 16:20], sm[:, s, 12:16], ACT.Exp).then_inc(sink_e, 1)

            def post_sq(l, which):
                for s in range(2):
                    q = 4 * l + 2 * which + s
                    if q < 6:
                        act.wait_ge(used, y_end(l, which))
                        src, dst = ps[:, 2 + 2 * s:4 + 2 * s, :], junk.rearrange("p (a b) -> p a b", a=2)
                    else:
                        src, dst = acc[s], junk
                    if s:
                        act.wait_ge(psq, q)
                    act.activation(dst, src, ACT.Square, accum_out=stat[:, 24 + 3 * q:25 + 3 * q]).then_inc(psq, 1)

            def gate_rows(l, which, s):
                q = 4 * l + 2 * which + s
                act.wait_ge(gb, q + 1)
                act.activation(xn[:, s, :].rearrange("p (a b) -> p a b", a=2), ps[:, 0:2, :], ACT.Copy).then_inc(gbs, 1)

            def ffn():
                split_to(FFN_U + 2)

                def silu(gu_end):
                    act.wait_ge(used, gu_end)
                    act.activation(sil.rearrange("p (s n) -> p s n", s=2), ps[:, 6:8, 0:256], ACT.Silu).then_inc(f_sil, 1)

                def h_round(f):
                    act.wait_ge(f_T, f + 1)
                    act.activation(h_hi[:, :].rearrange("p (s n) -> p s n", s=2), ps[:, 0:2, 0:256], ACT.Copy).then_inc(f_hi, 1)

                silu(FFN_U + 2)
                with act.Fori(0, (NFF - 1) // 2) as i:
                    for k in range(2):
                        c = FFN_U + 2 + 3 * k
                        hi(i, c)
                        hi(i, c + 1)
                        h_round(2 * i + k)
                        hi(i, c + 2)
                        silu(6 * i + c + 2)
                split[0] = FFN_U + 2 + 3 * (NFF - 1)
                split_to(FFN_U + 3 * NFF)
                h_round(NFF - 1)

            def route():
                act.wait_ge(r_rowT, 1)
                act.activation(hrow[0].rearrange("p (a b) -> p a b", a=2), ps[:, 0:2, :], ACT.Copy).then_inc(r_row, 1)
                act.wait_ge(r_diff, 1)
                act.activation(rt[:, 11, 8:10], rt[:, 11, 6:8], ACT.Exp).then_inc(r_exp, 1)
                act.activation(rt[:, 9, 0:1], rt[:, 11, 6:7], ACT.Copy).then_inc(m_sil, 1)

            def gathered_hi(n):
                act.wait_ge(m_gath, n + 1)
                act.activation(x_hi[:, 0, :].rearrange("p (a b) -> p a b", a=2), ps[:, 4:6, :], ACT.Copy).then_inc(m_xhi, 1)

            def moe(p):
                b = MOE_U + 42 * NE * p

                def silu(gu_end):
                    act.wait_ge(used, gu_end)
                    act.activation(sil, ps[:, 6, :], ACT.Silu).then_inc(m_sil, 1)

                def h_round(n):
                    act.wait_ge(m_T, n + 1)
                    act.activation(h_hi[:, :], ps[:, 0, :], ACT.Copy).then_inc(m_hi, 1)

                def y_half(e):
                    act.wait_ge(used, 42 * e + (b + 42))
                    act.activation(y_sb[:, 0:512], ps[:, 2, :], ACT.Copy).then_inc(m_y0, 1)

                def expert(e, first):
                    n0 = 7 * e + 56 * p
                    hi(7 * e, b)
                    hi(7 * e, b + 1)
                    if not first:
                        y_half(e - 1)
                    for k in range(2, 6):
                        hi(7 * e, b + k)
                    silu(42 * e + (b + 4))
                    hi(7 * e, b + 6)
                    act.wait_ge(m_bT, e + (8 * p + 1))
                    if not first:
                        act.wait_ge(m_c, 2 * e + 16 * p)
                    elif p:
                        act.wait_ge(m_c, 16 * p)
                    act.activation(back, ps[:, 1, 0:256].rearrange("p (s c) -> p s c", s=2), ACT.Copy).then_inc(m_back, 1)
                    h_round(n0)
                    for k in range(3, 6):
                        hi(7 * e, b + 4 + k)
                    silu(42 * e + (b + 8))
                    with act.Fori(2, NJ) as j:
                        for k in range(3):
                            hi(7 * e + (j - 1), b + 4 + k)
                        h_round(n0 + j - 1)
                        for k in range(3, 6):
                            hi(7 * e + (j - 1), b + 4 + k)
                        silu(42 * e + 6 * j + (b + 2))
                    hi(7 * e, b + 40)
                    hi(7 * e, b + 41)
                    h_round(n0 + (NJ - 1))
                    gathered_hi(e + (9 * p + 1))

                gathered_hi(9 * p)
                expert(0, True)
                with act.Fori(1, NE) as e:
                    expert(e, False)
                y_half(NE - 1)

            for l in range(DEPTH):
                if l == 0:
                    split_to(2)
                norm_rows(l, 0)
                for c in range(4):
                    split_to(ada_u(l, c) + 3)
                    rows(l, c)
                split_to(win_u(l, 0) + 2)
                norm_hi(l, 0)
                if l:
                    act.wait_ge(out_ctx[l - 1], NOUT)
                for j in range(NWIN):
                    split_to(win_u(l, j) + 3)
                    act.wait_ge(used, win_end(l, j))
                    for dst, src in proj_copies(0, j):
                        last = act.activation(dst, src, ACT.Copy)
                    last.then_inc(win_evac[0], 1)
                act.wait_ge(win_evac[0], NWIN * (l + 1))
                for s in range(2):
                    if s:
                        act.wait_ge(win_evac[1], NWIN * (l + 1))
                    o, r = 192 * s, 48 + 6 * (2 * l + s)
                    act.activation(xn[:, 0, o:o + QR], proj[s][:, CQ:CQ + QR], ACT.Square, accum_out=stat[:, r:r + 1])
                    act.activation(otmp[:, 128 * s:128 * s + P], proj[s][:, CKV:CKV + P], ACT.Square,
                                   accum_out=stat[:, r + 1:r + 2]).then_inc(csq, 1)
                    if s == 0:
                        act.activation(kp4[0].rearrange("p (h d) -> p h d", h=4),
                                       proj[0][:, KPE:KPE + 32].unsqueeze(1).to_broadcast([P, 4, 32]), ACT.Copy).then_inc(kp4_ready[0], 1)
                act.wait_ge(lam_s, l + 1)
                act.activation(lam[:, 2:4], lam[:, 0:2], ACT.Exp).then_inc(lam_e, 1)
                for k in range(np_(0)):
                    prep(l, k)
                    if k in (3, 5, 7):
                        split_to(ada_u(l, 4) + (k + 1) // 2)
                    if k == 6:
                        rows(l, 4)
                split_to(ada_u(l, 6) + 1)
                rows(l, 5)
                for i in range(10):
                    exps(l, i)
                    if i in (2, 4, 6, 8):
                        rows(l, 5 + i // 2)
                    if i < 7:
                        split_to(ada_u(l, 6) + i + 2)
                split_to(wo_u(l, 1))
                for s in range(2):
                    act.wait_ge(oT, 2 * l + s + 1)
                    act.activation(x_hi[:, s, :].rearrange("p (a b) -> p a b", a=2), ps[:, 4 * s:4 * s + 2, :],
                                   ACT.Copy).then_inc(o_hi, 1)
                split_to(wo_u(l, 1) + 1)
                gate_rows(l, 0, 0)
                split_to(ada_u(l, 11))
                post_sq(l, 0)
                gate_rows(l, 0, 1)
                rows(l, 10)
                norm_rows(l, 1)
                split_to(ada_u(l, 12))
                if l == 0:
                    norm_hi(l, 1)
                rows(l, 11)
                if l == 0:
                    ffn()
                    post_sq(0, 1)
                    gate_rows(0, 1, 0)
                    gate_rows(0, 1, 1)
                    split_to(ada_u(1, 1))

            route()
            moe(0)
            act.wait_ge(r_ready, 1)
            n = act.value_load(flag[0:1, 0:1], min_val=0, max_val=2 * P)
            with act.If(n > CAP):
                moe(1)
            gate_rows(1, 1, 0)
            act.wait_ge(m_done, 1)
            post_sq(1, 1)
            gate_rows(1, 1, 1)

        @block.vector
        def _(dve):
            steps, split = [0], [0]

            def link(i):
                steps[0] += 1
                i.then_inc(dve_step, 1)
                dve.wait_ge(dve_step, steps[0])

            def lo(t, c):
                dve.wait_ge(hi_done, 6 * t + (c + 1))
                if c >= NSPL:
                    dve.wait_ge(used, 6 * t + (c - NSPL + 1))
                n = slice(0, width(c))
                dve.tensor_sub(split_lo(c, n), raw[:, c % NRAW, n], split_hi(c, n)).then_inc(lo_done, 1)

            def split_to(end):
                for u in range(split[0], end):
                    lo(0, u)
                split[0] = max(split[0], end)

            def b2(v, n):
                return v.unsqueeze(2).to_broadcast([P, v.shape[1], n])

            dve.memset(cond[:, :, :].bitcast(F32), 0.0).then_inc(cond_ready, 1)
            dve.wait_ge(cond_ready, 1)
            dve.wait_ge(cond_T, 1)
            cT = ps[:, 6, 0:16].rearrange("p (s k) -> p k s", s=2)
            link(dve.tensor_copy(cond[:, :, 0:2], cT))
            dve.tensor_sub(cond[:, :, 2:4], cT, cond[:, :, 0:2]).then_inc(cond_ready, 1)

            def init_columns():
                dve.wait_ge(init_T, 1)
                dve.tensor_copy(gcol[:, :, :, :], ps[:, 6, 256:320].rearrange("p (a l k) -> p a l k", a=4, l=DEPTH))
                dve.tensor_copy(bcol[:, :, :, :], ps[:, 6, 384:480].rearrange("p (l a k) -> p l a k", l=DEPTH, a=6)).then_inc(init_cols, 1)
                dve.wait_ge(init_cols, 1)

            def section(l, k):
                n = 6 * l + k
                dve.wait_ge(col_mm, n + 1)
                src = ada_ps(k).rearrange("p (k s) -> p k s", s=2)
                if k % 3 == 0:
                    dve.tensor_tensor(mod[:, l, k, :, :], src, b2(bcol[:, l, k, :], 2), ALU.add).then_inc(mod_ready, 1)
                else:
                    link(dve.tensor_tensor(mtmp[:, :, :], src, b2(bcol[:, l, k, :], 2), ALU.add))
                    g = gcol[:, {1: 0, 2: 1, 4: 2, 5: 3}[k], l, :]
                    dve.scalar_tensor_tensor(out=mod[:, l, k, :, :], in0=mtmp[:, :, :], scalar=1.0 if k % 3 == 1 else 0.0,
                                             in1=b2(g, 2), op0=ALU.add, op1=ALU.mult).then_inc(mod_ready, 1)
                dve.wait_ge(mod_ready, n + 1)

            def diagonals(l, which):
                for s in range(2):
                    g = mod[:, l, 3 * which + 2, :, s]
                    dve.tensor_tensor(gdiag(4 * l + 2 * which + s).rearrange("p (k n) -> p k n", k=KT),
                                      cst[:, C_ID:C_ID + P].unsqueeze(1).to_broadcast([P, KT, P]), b2(g, P),
                                      ALU.mult).then_inc(diag_ready, 1)

            def norm_cols(l, which):
                if which:
                    dve.wait_ge(out_ctx[l], NOUT)
                for s in range(2):
                    q = 4 * l + 2 * which + s
                    h = h_of(l, which)[s].rearrange("p (k t) -> p k t", k=KT)
                    dve.wait_ge(nT, q + 1)
                    link(dve.tensor_tensor(h, ps[:, 2 * s:2 * s + 2, :].rearrange("p a (b t) -> p (a b) t", t=P),
                                           b2(mod[:, l, 3 * which + 1, :, s], P), ALU.mult))
                    dve.tensor_tensor(h, h, b2(mod[:, l, 3 * which, :, s], P), ALU.add).then_inc(nh, 1)
                if (l, which) == (1, 1):
                    return
                for s in range(2):
                    dve.wait_ge(nhi, 4 * l + 2 * which + s + 1)
                    dve.tensor_sub(x_lo[:, s, :], h_of(l, which)[s], x_hi[:, s, :]).then_inc(nlo, 1)

            def rope(v, g, w):
                cc, sc = (C_COS64, C_SIN64) if w == 64 else (C_COS32, C_SIN32)
                n = g * w
                t1, t2 = xn[:, 1, 0:n], xn[:, 1, 512:512 + n]
                cos = cst[:, cc:cc + w].unsqueeze(1).to_broadcast([P, g, w])
                sin = cst[:, sc:sc + w].rearrange("p (a b m) -> p a b m", a=2, b=2)
                v4 = v.rearrange("p (g a b m) -> p g a b m", g=g, a=2, b=2)
                t4 = t2.rearrange("p (g a b m) -> p g a b m", g=g, a=2, b=2)
                for a in range(2):
                    for h in range(2):
                        dve.tensor_tensor(t4[:, :, a, h, :], v4[:, :, a, 1 - h, :],
                                          sin[:, a, h, :].unsqueeze(1).to_broadcast([P, g, w // 4]), ALU.mult)
                link(dve.tensor_tensor(t1.rearrange("p (g w) -> p g w", g=g), v.rearrange("p (g w) -> p g w", g=g), cos, ALU.mult))
                return dve.tensor_tensor(v, t1, t2, ALU.add)

            def prep(l, k):
                step, b = PREP[1][k], 2 * (k % 3) + 1
                dve.wait_ge(prep_mm[1], np_(1) * l + k + 1)
                if l == 0 and k == 0:
                    dve.wait_ge(qz_zero, 1)
                if step == "BM":
                    mask = cst[:, C_MASK:C_MASK + P].unsqueeze(1).to_broadcast([P, 4, P])
                    dve.tensor_tensor(bm.rearrange("p (h k) -> p h k", h=4), ps[:, b, :].rearrange("p (h k) -> p h k", h=4),
                                      mask, ALU.add).then_inc(prep_evac[1], 1)
                    return
                for dst, src in prep_copies(1, step, b):
                    last = dve.tensor_copy(dst, src)
                last.then_inc(prep_evac[1], 1)
                if step == "C2":
                    dve.wait_ge(prep_evac[1], np_(1) * l + k + 1)
                    rope_small(small[:, P:2 * P]).then_inc(qr_ready, 1)

            def rope_small(v):
                t1, t2 = otmp[:, 0:P], otmp[:, P:2 * P]
                sin = cst[:, C_SIN32:C_SIN32 + 32].rearrange("p (a b m) -> p a b m", a=2, b=2)
                v4 = v.rearrange("p (g a b m) -> p g a b m", g=4, a=2, b=2)
                t4 = t2.rearrange("p (g a b m) -> p g a b m", g=4, a=2, b=2)
                for a in range(2):
                    for h in range(2):
                        dve.tensor_tensor(t4[:, :, a, h, :], v4[:, :, a, 1 - h, :],
                                          sin[:, a, h, :].unsqueeze(1).to_broadcast([P, 4, 8]), ALU.mult)
                link(dve.tensor_tensor(t1.rearrange("p (g w) -> p g w", g=4), v.rearrange("p (g w) -> p g w", g=4),
                                       cst[:, C_COS32:C_COS32 + 32].unsqueeze(1).to_broadcast([P, 4, 32]), ALU.mult))
                return dve.tensor_tensor(v, t1, t2, ALU.add)

            def soft_pre(l, i):
                it, s = ITEMS[i // 2], i % 2
                sc = SCALE[it]
                v = score_view(s)
                dve.wait_ge(scores, 10 * l + i + 1)
                mx, nb = sm[:, s, 0:4], sm[:, s, 4:8]
                if it == "D" and s == 1:
                    pv = probs[:, 1, :, :]
                    dve.scalar_tensor_tensor(out=pv[:, :, 0:P], in0=v[:, :, 0:P], scalar=sc,
                                             in1=bm.rearrange("p (h k) -> p h k", h=4), op0=ALU.mult, op1=ALU.add)
                    link(dve.tensor_scalar(pv[:, :, P:2 * P], v[:, :, P:2 * P], sc, None, ALU.mult))
                    link(dve.tensor_reduce(mx, pv, AX, ALU.max))
                    dve.tensor_scalar(nb, mx, -1.0, None, ALU.mult).then_inc(sm_bias, 1)
                    return
                link(dve.tensor_reduce(mx, v, AX, ALU.max))
                if it != "A":
                    dve.tensor_scalar(nb, mx, -sc, None, ALU.mult).then_inc(sm_bias, 1)
                    return
                sink = par[:, R_SINK:R_SINK + 4]
                link(dve.scalar_tensor_tensor(out=sm[:, s, 24:28], in0=mx, scalar=sc, in1=sink, op0=ALU.mult, op1=ALU.max))
                dve.tensor_scalar(nb, sm[:, s, 24:28], -1.0, None, ALU.mult).then_inc(sm_bias, 1)
                dve.tensor_sub(sm[:, s, 12:16], sink, sm[:, s, 24:28]).then_inc(sink_d, 1)

            def soft_T(l, i):
                s = i % 2
                dve.wait_ge(pT, 10 * l + i + 1)
                for kb in range(1 + s):
                    last = dve.tensor_copy(pt_sb[kb], ps[:, kb, :])
                last.then_inc(pt_evac, 1)
                if ITEMS[i // 2] == "A":
                    dve.wait_ge(sink_e, 2 * l + s + 1)
                    link(dve.tensor_add(sm[:, s, 8:12], sm[:, s, 8:12], sm[:, s, 16:20]))
                link(dve.reciprocal(sm[:, s, 20:24], sm[:, s, 8:12]))

            def soft_out(l, i):
                it, s = ITEMS[i // 2], i % 2
                n = 10 * l + i + 1
                dve.wait_ge(o_mm, n)
                o = ps[:, 2 + 2 * s, 0:256].rearrange("p (h d) -> p h d", h=4)
                r = b2(sm[:, s, 20:24], HD)
                if it not in ("B0", "B1"):
                    dve.tensor_tensor(xn[:, s, O_COL[it]:O_COL[it] + 256].rearrange("p (h d) -> p h d", h=4), o, r,
                                      ALU.mult).then_inc(o_evac, 1)
                    return
                t = otmp[:, :].rearrange("p (h m d) -> p h m d", h=2, m=2)
                dve.tensor_tensor(otmp[:, :].rearrange("p (h d) -> p h d", h=4), o, r, ALU.mult).then_inc(o_evac, 1)
                dve.wait_ge(o_evac, n)
                ob = xn[:, s, O_COL[it]:O_COL[it] + P].rearrange("p (h d) -> p h d", h=2)
                link(dve.scalar_tensor_tensor(out=ob, in0=t[:, :, 1, :], scalar=lam[:, 4:5], in1=t[:, :, 0, :],
                                              op0=ALU.mult, op1=ALU.add))
                if it == "B1":
                    o4 = xn[:, s, 256:512]
                    link(dve.tensor_mul(otmp[:, :], o4, o4))
                    st = 72 + 12 * (2 * l + s)
                    dve.tensor_reduce(stat[:, st:st + 4], otmp[:, :].rearrange("p (h d) -> p h d", h=4), AX,
                                      ALU.add).then_inc(dsq, 1)

            def residual(l, which):
                for s in range(2):
                    q = 4 * l + 2 * which + s
                    dve.wait_ge(prs, q + 1)
                    dve.wait_ge(gbs, q + 1)
                    y = ps[:, 2 + 2 * s:4 + 2 * s, :] if q < 6 else acc[s].rearrange("p (a b) -> p a b", a=2)
                    g = xn[:, s, :].rearrange("p (a b) -> p a b", a=2)
                    link(dve.scalar_tensor_tensor(out=g, in0=y, scalar=stat[:, 26 + 3 * q:27 + 3 * q], in1=g,
                                                  op0=ALU.mult, op1=ALU.mult))
                    dve.tensor_add(x[:, s, :], x[:, s, :], xn[:, s, :]).then_inc(x_upd, 1)

            def ffn():
                split_to(FFN_U + 2)

                def hidden(f):
                    dve.wait_ge(f_sil, f + 1)
                    dve.tensor_mul(hid.rearrange("p (s n) -> p s n", s=2), ps[:, 6:8, 256:512],
                                   sil.rearrange("p (s n) -> p s n", s=2)).then_inc(f_h, 1)

                def h_rest(f):
                    dve.wait_ge(f_hi, f + 1)
                    dve.tensor_sub(h_lo[:, :].rearrange("p (s n) -> p s n", s=2), ps[:, 0:2, 0:256],
                                   h_hi[:, :].rearrange("p (s n) -> p s n", s=2)).then_inc(f_lo, 1)

                hidden(0)
                with dve.Fori(0, (NFF - 1) // 2) as i:
                    for k in range(2):
                        c = FFN_U + 2 + 3 * k
                        lo(i, c)
                        lo(i, c + 1)
                        h_rest(2 * i + k)
                        lo(i, c + 2)
                        hidden(2 * i + (k + 1))
                split[0] = FFN_U + 2 + 3 * (NFF - 1)
                split_to(FFN_U + 3 * NFF)
                h_rest(NFF - 1)

            def route():
                R = [rt[:, i, :].rearrange("p (s e) -> p s e", s=2) for i in range(8)]
                col = [rt[:, 11, 2 * i:2 * i + 2] for i in range(8)]
                logit, eq, sel1, sel2, rest, mask, wt, tmp = R
                m1, t, m2, dm, ex, g1, g2, mx = col
                rev = cst[:, C_REV8:C_REV8 + 8].unsqueeze(1).to_broadcast([P, 2, NE])

                def first_max(sel, v, m):
                    link(dve.tensor_reduce(m, v, AX, ALU.max))
                    link(dve.tensor_tensor(eq, v, b2(m, NE), ALU.is_equal))
                    link(dve.tensor_tensor(eq, eq, rev, ALU.mult))
                    link(dve.tensor_reduce(t, eq, AX, ALU.max))
                    link(dve.tensor_tensor(sel, eq, b2(t, NE), ALU.is_equal))

                dve.wait_ge(r_rowT, 2)
                dve.tensor_copy(hrow[1].rearrange("p (a b) -> p a b", a=2), ps[:, 2:4, :]).then_inc(r_row, 1)
                dve.wait_ge(r_mm, 1)
                link(dve.tensor_copy(logit, ps[:, 4, 0:16].rearrange("p (s e) -> p s e", s=2)))
                first_max(sel1, logit, m1)
                link(dve.scalar_tensor_tensor(out=rest, in0=sel1, scalar=-3.0e38, in1=logit, op0=ALU.mult, op1=ALU.add))
                first_max(sel2, rest, m2)
                link(dve.tensor_add(mask, sel1, sel2))
                dve.tensor_sub(dm, m2, m1).then_inc(r_diff, 1)
                dve.wait_ge(r_exp, 1)
                link(dve.tensor_scalar(tmp[:, 0, 0:2], ex, 1.0, None, ALU.add))
                link(dve.reciprocal(g1, tmp[:, 0, 0:2]))
                link(dve.tensor_mul(g2, ex, g1))
                link(dve.tensor_tensor(wt, sel1, b2(g1, NE), ALU.mult))
                link(dve.tensor_tensor(tmp, sel2, b2(g2, NE), ALU.mult))
                link(dve.memset(comb[:, :, :], 0.0))
                link(dve.memset(pos[:, :, :, :], -1.0 - 2 * P))
                link(dve.tensor_add(comb[:, :, 0:NE], wt, tmp))
                dve.wait_ge(r_pos, 1)
                for s in range(2):
                    link(dve.scalar_tensor_tensor(out=tmp[:, s, :], in0=ps[:, 6, 8 * s:8 * s + 8], scalar=1.0,
                                                  in1=mask[:, s, :], op0=ALU.add, op1=ALU.mult))
                for p in range(2):
                    link(dve.tensor_scalar(pos[:, p, :, 0:NE], tmp, 1.0 + CAP * p, None, ALU.subtract))
                link(dve.tensor_reduce(mx[:, 0:1], ps[:, 6, 16:24], AX, ALU.max))
                dve.tensor_copy(flag[:, :], mx[:, 0:1]).then_inc(r_ready, 1)
                for s in range(2):
                    last = dve.memset(acc[s], 0.0)
                last.then_inc(m_h, 1)

            def picks(p, e):
                iota = cst[:, C_IOTA:C_IOTA + P]
                for s in range(2):
                    dve.tensor_scalar(pick[:, s, :], iota, pos[:, p, s, bass.ds(e, 1)], None, ALU.is_equal)
                    last = dve.tensor_scalar(pickw[:, s, :], iota, pos[:, p, s, bass.ds(e, 1)], comb[:, s, bass.ds(e, 1)],
                                             ALU.is_equal, ALU.mult)
                last.then_inc(m_pick, 1)

            def gathered_lo(n):
                dve.wait_ge(m_xhi, n + 1)
                dve.tensor_sub(x_lo[:, 0, :].rearrange("p (a b) -> p a b", a=2), ps[:, 4:6, :],
                               x_hi[:, 0, :].rearrange("p (a b) -> p a b", a=2)).then_inc(m_xlo, 1)

            def moe(p):
                b = MOE_U + 42 * NE * p

                def hidden(n):
                    dve.wait_ge(m_sil, n + 2)
                    dve.tensor_mul(hid, ps[:, 7, :], sil).then_inc(m_h, 1)

                def h_rest(n):
                    dve.wait_ge(m_hi, n + 1)
                    dve.tensor_sub(h_lo[:, :], ps[:, 0, :], h_hi[:, :]).then_inc(m_lo, 1)

                def y_half(e):
                    dve.wait_ge(used, 42 * e + (b + 42))
                    dve.tensor_copy(y_sb[:, 512:1024], ps[:, 3, :]).then_inc(m_y1, 1)

                def accumulate(e):
                    for s in range(2):
                        dve.wait_ge(m_c, 2 * e + (16 * p + s + 1))
                        a = acc[s].rearrange("p (a b) -> p a b", a=2)
                        dve.tensor_add(a, a, ps[:, 4 - 2 * s:6 - 2 * s, :]).then_inc(m_acc, 1)

                def expert(e, first):
                    n0 = 7 * e + 56 * p
                    lo(7 * e, b)
                    lo(7 * e, b + 1)
                    if not first:
                        y_half(e - 1)
                    for k in range(2, 5):
                        lo(7 * e, b + k)
                    if not first:
                        accumulate(e - 1)
                    lo(7 * e, b + 5)
                    hidden(n0)
                    lo(7 * e, b + 6)
                    lo(7 * e, b + 7)
                    h_rest(n0)
                    dve.wait_ge(m_bT, e + (8 * p + 1))
                    dve.wait_ge(m_gath, e + (9 * p + 1))
                    picks(p, e + 1)
                    lo(7 * e + 1, b + 2)
                    lo(7 * e + 1, b + 3)
                    hidden(n0 + 1)
                    with dve.Fori(2, NJ) as j:
                        for k in range(3):
                            lo(7 * e + (j - 1), b + 4 + k)
                        h_rest(n0 + j - 1)
                        for k in range(3, 6):
                            lo(7 * e + (j - 1), b + 4 + k)
                        hidden(n0 + j)
                    lo(7 * e, b + 40)
                    lo(7 * e, b + 41)
                    h_rest(n0 + (NJ - 1))
                    gathered_lo(e + (9 * p + 1))

                picks(p, 0)
                gathered_lo(9 * p)
                expert(0, True)
                with dve.Fori(1, NE) as e:
                    expert(e, False)
                y_half(NE - 1)
                accumulate(NE - 1)

            for l in range(DEPTH):
                lam_init = 0.8 - 0.6 * math.exp(-0.3 * l)
                if l == 0:
                    split_to(ada_u(0, 2))
                    init_columns()
                split_to(ada_u(l, 2) + 2)
                section(l, 0)
                split_to(win_u(l, 0) + 2)
                section(l, 1)
                norm_cols(l, 0)
                for j in range(NWIN):
                    split_to(win_u(l, j) + 3)
                    dve.wait_ge(used, win_end(l, j))
                    for dst, src in proj_copies(1, j):
                        last = dve.tensor_copy(dst, src)
                    last.then_inc(win_evac[1], 1)
                dve.wait_ge(win_evac[1], NWIN * (l + 1))
                dve.wait_ge(in_layer[l], N_LAYER)
                if l == 0:
                    dve.wait_ge(in_cst, 16)
                link(rope(proj[1][:, QA:QA + 384], 6, 64))
                link(rope(proj[1][:, QB:QB + 512], 16, 32))
                link(rope(proj[1][:, KPE:KPE + 32], 1, 32))
                dve.tensor_copy(kp4[1].rearrange("p (h d) -> p h d", h=4),
                                proj[1][:, KPE:KPE + 32].unsqueeze(1).to_broadcast([P, 4, 32])).then_inc(roped, 1)
                dve.tensor_copy(kp4[2].rearrange("p (h d) -> p h d", h=4),
                                kcache[:, K_KPE:K_KPE + 32].unsqueeze(1).to_broadcast([P, 4, 32])).then_inc(kp4_ready[1], 1)
                for s in range(2):
                    dve.wait_ge(crs, 2 * l + s + 1)
                    r = 48 + 6 * (2 * l + s)
                    for o, n, g, c in ((CQ, QR, R_QN, 4), (CKV, P, R_KVN, 5)):
                        v = proj[s][:, o:o + n]
                        last = dve.scalar_tensor_tensor(out=v, in0=v, scalar=stat[:, r + c:r + c + 1], in1=par[:, g:g + n],
                                                        op0=ALU.mult, op1=ALU.mult)
                    last.then_inc(cnorm, 1)
                dve.wait_ge(cnorm, 2 * l + 2)
                for i in range(2):
                    o = R_LAM + 64 * i
                    last = dve.tensor_tensor_reduce(out=xn[:, 1, 512 + 32 * i:544 + 32 * i], in0=par[:, o:o + 32], in1=par[:, o + 32:o + 64],
                                                    scale=1.0, scalar=0.0, op0=ALU.mult, op1=ALU.add, accum_out=lam[:, i:i + 1])
                last.then_inc(lam_s, 1)
                dve.wait_ge(lam_e, l + 1)
                link(dve.scalar_tensor_tensor(out=lam[:, 4:5], in0=lam[:, 3:4], scalar=-lam_init, in1=lam[:, 2:3],
                                              op0=ALU.add, op1=ALU.subtract))
                link(dve.tensor_scalar(par[:, R_SUB:R_SUB + 64], par[:, R_SUB:R_SUB + 64], 1.0 - lam_init, None, ALU.mult))
                for k in range(np_(1)):
                    prep(l, k)
                    if k in (3, 5, 7, 9):
                        split_to(ada_u(l, 4) + (k + 1) // 2)
                section(l, 2)
                soft_pre(l, 0)
                for i in range(10):
                    if i + 1 < 10:
                        soft_pre(l, i + 1)
                    soft_T(l, i)
                    if i < 7:
                        split_to(ada_u(l, 6) + i + 2)
                    if i in (4, 8):
                        section(l, 2 + i // 4)
                    soft_out(l, i)
                split_to(wo_u(l, 1))
                for s in range(2):
                    n = 2 * l + s
                    dve.wait_ge(drs, n + 1)
                    o4 = xn[:, s, 256:512].rearrange("p (h d) -> p h d", h=4)
                    st = 80 + 12 * n
                    link(dve.tensor_tensor(o4, o4, b2(stat[:, st:st + 4], HD), ALU.mult))
                    dve.tensor_tensor(o4, o4, par[:, R_SUB:R_SUB + 64].unsqueeze(1).to_broadcast([P, 4, HD]),
                                      ALU.mult).then_inc(o_ready, 1)
                for s in range(2):
                    dve.wait_ge(o_hi, 2 * l + s + 1)
                    dve.tensor_sub(x_lo[:, s, :].rearrange("p (a b) -> p a b", a=2), ps[:, 4 * s:4 * s + 2, :],
                                   x_hi[:, s, :].rearrange("p (a b) -> p a b", a=2)).then_inc(o_lo, 1)
                diagonals(l, 0)
                split_to(ada_u(l, 11))
                residual(l, 0)
                norm_cols(l, 1)
                split_to(ada_u(l, 12))
                section(l, 5)
                if l == 0:
                    diagonals(0, 1)
                    ffn()
                    residual(0, 1)

            route()
            moe(0)
            dve.wait_ge(r_ready, 1)
            n = dve.value_load(flag[0:1, 0:1], min_val=0, max_val=2 * P)
            with dve.If(n > CAP):
                moe(1)
            diagonals(1, 1)
            dve.memset(rt[:, 10, :], 0.0).then_inc(m_done, 1)
            residual(1, 1)

        @block.tensor
        def _(pe):
            def products(t, c, tiles):
                pe.wait_ge(hi_done, 6 * t + (c + 1))
                for out, xh, xl, w, start, stop in tiles:
                    pe.matmul(out, xh, split_hi(c, w), start=start, stop=False, skip_group_check=True)
                    last = pe.matmul(out, xl, split_hi(c, w), start=False, stop=False, skip_group_check=True)
                last.then_inc(hi_used, 1)
                pe.wait_ge(lo_done, 6 * t + (c + 1))
                for out, xh, xl, w, start, stop in tiles:
                    last = pe.matmul(out, xh, split_lo(c, w), start=False, stop=stop, skip_group_check=True)
                last.then_inc(used, 1)

            def xcols(s, k):
                return x_hi[:, s, P * k:P * k + P], x_lo[:, s, P * k:P * k + P]

            pe.wait_ge(in_cst, 16)
            pe.wait_ge(cond_silu, 1)
            pe.transpose(ps[:, 6, 0:16], rows_s, ident(16)).then_inc(cond_T, 1)

            def ada(l, n):
                c, h = n // 2, n % 2
                u, s = ada_u(l, c) + h, (ada_u(l, c) + h) % NSPL
                if h == 0 and (l or c):
                    pe.wait_ge(row_evac, 12 * l + c)
                for part, ready in ((w_hi, hi_done), (w_lo, lo_done)):
                    pe.wait_ge(ready, u + 1)
                    for kt in range(4):
                        last = pe.matmul(ps[0:CM, 7, :], cond[:, 4 * h + kt, :], part[:, s, 512 * kt:512 * kt + 512],
                                         start=h == 0 and kt == 0 and part is w_hi, stop=h == 1 and kt == 3 and part is w_lo)
                    last.then_inc(hi_used if part is w_hi else used, 1)

            def columns(l, k):
                n = 6 * l + k
                pe.wait_ge(row_evac, 2 * n + 2)
                if n:
                    pe.wait_ge(mod_ready, n)
                for kt in range(KT):
                    last = pe.matmul(ada_ps(k)[:, 2 * kt:2 * kt + 2], mrow[0:4, P * kt:P * kt + P], cst[0:4, C_SEL:C_SEL + 2],
                                     start=True, stop=True)
                last.then_inc(col_mm, 1)

            def cols(k, n):
                return slice(n * k, n * k + n)

            def norm_T(l, which):
                for s in range(2):
                    q = 4 * l + 2 * which + s
                    if q >= 2:
                        pe.wait_ge(gbs, q - q % 2)
                    pe.wait_ge(nxn, q + 1)
                    for k in range(KT):
                        last = pe.transpose(ps[:, 2 * s + k // 4, cols(k % 4, P)], xn[:, s, cols(k, P)], ident())
                    last.then_inc(nT, 1)

            def gates(l, which, s):
                q = 4 * l + 2 * which + s
                pe.wait_ge(diag_ready, q + 1)
                if s:
                    pe.wait_ge(gbs, q)
                for h in range(2):
                    last = pe.matmul(ps[:, h, :], cst[:, C_ONE:C_ONE + P], gdiag(q)[:, cols(h, 512)], start=True, stop=True)
                last.then_inc(gb, 1)

            def prep(l, k):
                for s in range(2):
                    if k >= np_(s):
                        continue
                    step, b, nk = PREP[s][k], 2 * (k % 3) + s, nk_of(s)
                    pj = proj[s]
                    if k >= 3:
                        pe.wait_ge(prep_evac[s], np_(s) * l + k - 2)
                    elif k == 0:
                        pe.wait_ge(win_evac[s], NWIN * (l + 1))
                        if s:
                            pe.wait_ge(roped, l + 1)
                            pe.wait_ge(in_layer[l], N_LAYER)
                    o = ps[:, b, :]

                    def T(c, src, n=P):
                        return pe.transpose(o[0:n, cols(c, P)], src, ident())

                    if step == "A":
                        T(0, pj[:, QA:QA + P])
                        T(1, pj[:, QA + P:QA + 2 * P])
                        last = T(2, pj[:, KA:KA + P])
                        if s:
                            last = T(3, kcache[:, K_WK:K_WK + P])
                    elif step in ("B0", "B1"):
                        h = P * int(step[1])
                        T(0, pj[:, QB + h:QB + h + P])
                        last = T(1, pj[:, KB + h:KB + h + P])
                        if s:
                            last = T(2, kcache[:, K_DK + h:K_DK + h + P])
                    elif step == "D":
                        for r in range(2):
                            T(r, pj[:, QD + P * r:QD + P * r + P])
                            last = T(2 + r, pj[:, KD + P * r:KD + P * r + P])
                    elif step == "Dc":
                        for r in range(2):
                            last = T(r, kcache[:, K_NK + P * r:K_NK + P * r + P])
                    elif step == "C1":
                        pe.wait_ge(cnorm, 2 * l + s + 1)
                        for r in range(2):
                            T(r, pj[:, CQ + 96 * r:CQ + 96 * r + 96], 96)
                        last = T(2, pj[:, CKV:CKV + P])
                        if s:
                            last = T(3, kcache[:, K_CKV:K_CKV + P])
                    elif step == "C2":
                        pe.wait_ge(prep_evac[s], np_(s) * l + k)
                        pe.wait_ge(in_layer[l], N_LAYER)
                        for r in range(3):
                            for i in range(2):
                                cq = ct[s][0:96, cols(i, P)]
                                if r < 2:
                                    last = pe.matmul(o[:, cols(r, P)], wuq[0:96, 384 * i + P * r:384 * i + P * r + P], cq, start=i == 0, stop=i == 1)
                                else:
                                    last = pe.matmul(o[:, cols(2, P)], cq, wuq[0:96, 384 * i + 256:384 * i + 384], start=i == 0, stop=i == 1)
                    elif step in ("C3", "C4"):
                        for r in range(2):
                            if step == "C3":
                                last = pe.matmul(o[:, 256 * r:256 * r + nk], wukv[:, cols(r, P)], ct[s][:, 256:256 + nk],
                                                 start=True, stop=True)
                            elif r <= s:
                                last = pe.matmul(o[:, cols(r, 256)], ct[s][:, 256 + P * r:384 + P * r], wukv[:, 256:512],
                                                 start=True, stop=True)
                    elif step == "C5":
                        pe.wait_ge(kp4_ready[s], l + 1)
                        if s:
                            pe.wait_ge(qr_ready, l + 1)
                        T(0, small[:, P * s:P * s + P])
                        last = T(1, kp4[s])
                        if s:
                            last = T(2, kp4[2])
                    else:
                        last = pe.matmul(o, cst[:, C_ANTI:C_ANTI + P], bm, start=True, stop=True)
                    last.then_inc(prep_mm[s], 1)

            def item_scores(l, i):
                it, s = ITEMS[i // 2], i % 2
                nk, v = nk_of(s), score_view(s)
                if i < 2:
                    for t in range(2):
                        pe.wait_ge(prep_evac[t], np_(t) * (l + 1))
                else:
                    pe.wait_ge(o_evac, 10 * l + i - 1)
                for h in range(4):
                    m = 2 * (h % 2) + h // 2 if it == "A" else h
                    k = nk * (KEYS[it] + (h // 2 if it in ("C", "D") else 0))
                    last = pe.matmul(v[:, h, :], qz[:, s, QZ[it], m, :], keys[s][:, k:k + nk], start=True, stop=it != "C")
                    if it == "C":
                        k = nk * KEYS["rope"]
                        last = pe.matmul(v[:, h, :], qz[:, s, QZ["rope"], h, :], keys[s][:, k:k + nk], start=False, stop=True)
                last.then_inc(scores, 1)

            def item_T(l, i):
                n = 10 * l + i
                pe.wait_ge(probs_ready, n + 1)
                if n:
                    pe.wait_ge(pt_evac, n)
                for kb in range(1 + i % 2):
                    for h in range(4):
                        last = pe.transpose(ps[:, kb, cols(h, P)], probs[:, i % 2, h, cols(kb, P)], ident())
                last.then_inc(pT, 1)

            def item_out(l, i):
                it, s = ITEMS[i // 2], i % 2
                pe.wait_ge(pt_evac, 10 * l + i + 1)
                for h in range(4):
                    if it == "A":
                        vs = (proj[s][:, VA + HD * (h // 2):VA + HD * (h // 2) + HD],
                              vcache[:, V_W + HD * (h // 2):V_W + HD * (h // 2) + HD])
                    elif it == "D":
                        vs = (proj[s][:, VD + HD * h:VD + HD * h + HD], vcache[:, V_N + HD * h:V_N + HD * h + HD])
                    elif it == "C":
                        vs = [v_mla[s][:, cols(4 * kb + h, HD)] for kb in range(1 + s)]
                    else:
                        g = 2 * int(it[1]) + h // 2
                        vs = (proj[s][:, VB + HD * g:VB + HD * g + HD], vcache[:, V_D + HD * g:V_D + HD * g + HD])
                    for kb in range(1 + s):
                        last = pe.matmul(ps[:, 2 + 2 * s, cols(h, HD)], pt_sb[kb][:, cols(h, P)], vs[kb],
                                         start=kb == 0, stop=kb == s)
                last.then_inc(o_mm, 1)

            def attention(l):
                for k in range(np_(1)):
                    prep(l, k)
                    if k in (3, 5, 7, 9):
                        ada(l, 8 + (k - 3) // 2)
                columns(l, 2)
                item_scores(l, 0)
                for i in range(10):
                    if i + 1 < 10:
                        item_scores(l, i + 1)
                    item_T(l, i)
                    if i in (4, 8):
                        columns(l, 2 + i // 4)
                    if i < 8:
                        ada(l, 12 + i)
                    item_out(l, i)

            def out_projection(l):
                for s in range(2):
                    pe.wait_ge(o_ready, 2 * l + s + 1)
                    if s == 0:
                        pe.wait_ge(pt_evac, 10 * (l + 1))
                    else:
                        pe.wait_ge(o_evac, 10 * (l + 1))
                    for k in range(KT):
                        last = pe.transpose(ps[:, 4 * s + k // 4, cols(k % 4, P)], xn[:, s, cols(k, P)], ident())
                    last.then_inc(oT, 1)
                pe.wait_ge(o_evac, 10 * (l + 1))
                pe.wait_ge(o_hi, 2 * l + 2)
                pe.wait_ge(o_lo, 2 * l + 2)
                for j in range(2):
                    for h in range(2):
                        tiles = [(ps[:, 2 + 2 * s + j, :], *xcols(s, 4 * h + k), cols(k, 512), h == 0 and k == 0, h == 1 and k == 3)
                                 for s in range(2) for k in range(4)]
                        products(0, wo_u(l, j) + h, tiles)
                    gates(l, 0, j)

            def dense():
                def gate_up(t, c, up):
                    products(t, c, [(ps[:, 6 + s, 256 * up:256 * up + 256], *xcols(s, k), cols(k, 256), k == 0, k == KT - 1)
                                    for s in range(2) for k in range(KT)])

                def hidden_T(f):
                    pe.wait_ge(f_h, f + 1)
                    for s in range(2):
                        for r in range(2):
                            last = pe.transpose(ps[:, s, cols(r, P)], hid[:, 256 * s + P * r:256 * s + P * r + P], ident())
                    last.then_inc(f_T, 1)

                def down(t, c, f, first=False, final=False):
                    pe.wait_ge(f_hi, f + 1)
                    pe.wait_ge(f_lo, f + 1)
                    products(t, c, [(ps[:, 2 + 2 * s + n, :], h_hi[:, 256 * s + P * r:256 * s + P * r + P],
                                     h_lo[:, 256 * s + P * r:256 * s + P * r + P], slice(1024 * r + 512 * n, 1024 * r + 512 * n + 512),
                                     first and r == 0, final and r == 1)
                                    for s in range(2) for r in range(2) for n in range(2)])

                def two_blocks(i, first):
                    for k in range(2):
                        c = FFN_U + 2 + 3 * k
                        pe.wait_ge(f_h, 2 * i + (k + 1))
                        gate_up(i, c, 0)
                        hidden_T(2 * i + k)
                        gate_up(i, c + 1, 1)
                        down(i, c + 2, 2 * i + k, first=first and k == 0)

                for s in range(2):
                    pe.wait_ge(nhi, 2 + s + 1)
                    pe.wait_ge(nlo, 2 + s + 1)
                gate_up(0, FFN_U, 0)
                gate_up(0, FFN_U + 1, 1)
                two_blocks(0, True)
                with pe.Fori(1, (NFF - 1) // 2) as i:
                    two_blocks(i, False)
                hidden_T(NFF - 1)
                down(0, FFN_U + 3 * NFF - 1, NFF - 1, final=True)

            def route():
                pe.wait_ge(in_rtr, 16)
                for s in range(2):
                    pe.wait_ge(nh, 6 + s + 1)
                for s in range(2):
                    for k in range(KT):
                        last = pe.matmul(ps[:, 4, cols(s, NE)], hT[s][:, cols(k, P)], rtr[:, k, :], start=k == 0, stop=k == KT - 1)
                last.then_inc(r_mm, 1)
                for s in range(2):
                    for k in range(KT):
                        last = pe.transpose(ps[:, 2 * s + k // 4, cols(k % 4, P)], hT[s][:, cols(k, P)], ident())
                    last.then_inc(r_rowT, 1)
                pe.wait_ge(r_diff, 1)
                up, one = cst[:, C_UP:C_UP + P], cst[:, C_ONE:C_ONE + P]
                mask = [rt[:, 5, cols(s, NE)] for s in range(2)]
                for n, pair in enumerate(((up, None), (one, up), (one, one))):
                    for s, m in enumerate(pair):
                        if m is not None:
                            last = pe.matmul(ps[:, 6, cols(n, NE)], m, mask[s], start=s == 0, stop=s == 1 or pair[1] is None)
                last.then_inc(r_pos, 1)

            def moe(p):
                b = MOE_U + 42 * NE * p

                def gather(n):
                    pe.wait_ge(m_pick, n + (9 * p + 1))
                    for k in range(KT):
                        for s in range(2):
                            last = pe.matmul(ps[:, 4 + k // 4, cols(k % 4, P)], hrow[s][:, cols(k, P)], pick[:, s, :],
                                             start=s == 0, stop=s == 1)
                    last.then_inc(m_gath, 1)

                def gate_up(t, c, up):
                    for h in range(2):
                        products(t, c + h, [(ps[:, 6 + up, :], *xcols(0, 4 * h + k), cols(k, 512), h == 0 and k == 0, h == 1 and k == 3)
                                            for k in range(4)])

                def hidden_T(n):
                    pe.wait_ge(m_h, n + 2)
                    for r in range(4):
                        last = pe.transpose(ps[:, 0, cols(r, P)], hid[:, cols(r, P)], ident())
                    last.then_inc(m_T, 1)

                def down(t, c, n, first=False, final=False):
                    pe.wait_ge(m_hi, n + 1)
                    pe.wait_ge(m_lo, n + 1)
                    for h in range(2):
                        products(t, c + h, [(ps[:, 2 + q, :], h_hi[:, cols(2 * h + r, P)], h_lo[:, cols(2 * h + r, P)],
                                             slice(1024 * r + 512 * q, 1024 * r + 512 * q + 512),
                                             first and h == 0 and r == 0, final and h == 1 and r == 1)
                                            for r in range(2) for q in range(2)])

                def combine(e):
                    pe.wait_ge(m_y0, e + (8 * p + 1))
                    pe.wait_ge(m_y1, e + (8 * p + 1))
                    pe.wait_ge(m_back, e + (8 * p + 1))
                    for s in range(2):
                        for h in range(2):
                            last = pe.matmul(ps[:, 4 - 2 * s + h, :], back[:, s, :], y_sb[:, cols(h, 512)], start=True, stop=True)
                        last.then_inc(m_c, 1)

                def expert(e, first):
                    n0 = 7 * e + 56 * p
                    pe.wait_ge(m_xhi, e + (9 * p + 1))
                    pe.wait_ge(m_xlo, e + (9 * p + 1))
                    pe.wait_ge(m_sil, n0 + 1)
                    gate_up(7 * e, b, 0)
                    pe.wait_ge(m_h, n0 + 1)
                    gate_up(7 * e, b + 2, 1)
                    if not first:
                        combine(e - 1)
                    for t in range(2):
                        last = pe.transpose(ps[:, 1, cols(t, P)], pickw[:, t, :], ident())
                    last.then_inc(m_bT, 1)
                    pe.wait_ge(m_sil, n0 + 2)
                    gate_up(7 * e, b + 4, 0)
                    hidden_T(n0)
                    gate_up(7 * e + 1, b, 1)
                    if not first:
                        pe.wait_ge(m_acc, 2 * e + 16 * p)
                    elif p:
                        pe.wait_ge(m_acc, 16 * p)
                    down(7 * e + 1, b + 2, n0, first=True)
                    with pe.Fori(2, NJ) as j:
                        pe.wait_ge(m_sil, n0 + j + 1)
                        gate_up(7 * e + (j - 1), b + 4, 0)
                        hidden_T(n0 + j - 1)
                        gate_up(7 * e + j, b, 1)
                        down(7 * e + j, b + 2, n0 + j - 1)
                    hidden_T(n0 + (NJ - 1))
                    gather(e + 1)
                    down(7 * e, b + 40, n0 + (NJ - 1), final=True)

                if p == 0:
                    pe.wait_ge(r_row, 2)
                else:
                    pe.wait_ge(m_acc, 16)
                gather(0)
                expert(0, True)
                with pe.Fori(1, NE) as e:
                    expert(e, False)
                combine(NE - 1)

            for l in range(DEPTH):
                if l:
                    gates(0, 1, 0)
                    gates(0, 1, 1)
                if l == 0:
                    pe.wait_ge(cond_ready, 2)
                for n in range(8):
                    ada(l, n)
                    if n == 3 and l == 0:
                        pe.wait_ge(in_g, 80)
                        pe.transpose(ps[:, 6, 256:320], rows_g, ident(64))
                        pe.transpose(ps[:, 6, 384:480], rows_b, ident(96)).then_inc(init_T, 1)
                    if n == 4:
                        if l == 0:
                            pe.wait_ge(init_cols, 1)
                        columns(l, 0)
                norm_T(l, 0)
                columns(l, 1)
                for s in range(2):
                    pe.wait_ge(nhi, 4 * l + s + 1)
                    pe.wait_ge(nlo, 4 * l + s + 1)
                for j in range(NWIN):
                    if j >= 2:
                        for s in range(2):
                            pe.wait_ge(win_evac[s], NWIN * l + j - 1)
                    for h in range(2):
                        products(0, win_u(l, j) + h,
                                 [(ps[:, 2 + 2 * (j % 2) + s, 0:WIN_N], *xcols(s, 4 * h + k), cols(k, WIN_N),
                                   h == 0 and k == 0, h == 1 and k == 3) for s in range(2) for k in range(4)])
                attention(l)
                out_projection(l)
                ada(l, 20)
                ada(l, 21)
                norm_T(l, 1)
                ada(l, 22)
                ada(l, 23)
                columns(l, 5)
                if l == 0:
                    pe.wait_ge(mod_ready, 6)
                    dense()
                    pe.wait_ge(f_lo, NFF)
                    pe.wait_ge(f_h, NFF)

            route()
            moe(0)
            pe.wait_ge(r_ready, 1)
            n = pe.value_load(flag[0:1, 0:1], min_val=0, max_val=2 * P)
            with pe.If(n > CAP):
                moe(1)
            gates(1, 1, 0)
            gates(1, 1, 1)


_INS = ["x_prompt", "x_sample", "cache_win_k", "cache_win_v", "cache_diff_k", "cache_diff_v", "cache_mla_ckv",
        "cache_mla_kpe", "cache_na_k", "cache_na_v", "c", "c_ctx", "w_ada", "b_ada", "norm_mix_pre", "norm_mix_post",
        "norm_ffn_pre", "norm_ffn_post", "w_in", "w_o", "win_sink", "diff_lq1", "diff_lk1", "diff_lq2", "diff_lk2",
        "diff_subln", "mla_q_norm", "mla_kv_norm", "mla_wuq", "mla_wukv", "na_rpb", "ffn_w_gate", "ffn_w_up",
        "ffn_w_down", "moe_router", "moe_w_gate", "moe_w_up", "moe_w_down"]
_OUTS = [(1, P, D), (1, P, D), (1, DEPTH, 2, P, HD), (1, DEPTH, 2, P, HD), (1, DEPTH, 4, P, HD), (1, DEPTH, 4, P, HD),
         (1, DEPTH, P, P), (1, DEPTH, P, 32), (1, DEPTH, 4, P, HD), (1, DEPTH, 4, P, HD)]


def kernel(**inputs):
    import concourse.bacc as _bacc
    from concourse.bass_utils import run_bass_kernel_spmd as _run

    nc = _bacc.Bacc("TRN2", target_bir_lowering=False, num_devices=1)
    arrays, ins, outs = {}, [], []
    for name in _INS + ["constants"]:
        a = constants() if name == "constants" else np.ascontiguousarray(inputs[name])
        arrays[f"in_{name}"] = a
        ins.append(nc.dram_tensor(f"in_{name}", a.shape, mybir.dt.from_np(a.dtype), kind="ExternalInput").ap())
    for i, shape in enumerate(_OUTS):
        outs.append(nc.dram_tensor(f"out_{i}", shape, F32, kind="ExternalOutput").ap())
    program(nc, ins, outs)
    r = _run(nc, [arrays], core_ids=[0])
    return tuple(r.results[0][f"out_{i}"] for i in range(len(_OUTS)))
```
